# Optimizing a Trainium2 kernel written in Bass

```python
import numpy as np
import jax
import jax.numpy as jnp
from jax import lax

D_MODEL = 1024
BATCH = 1
SEQ = 512
DEPTH = 2
DEC_BATCH = 8
DEC_SEQ = 4
PAST_LEN = 4096
PAGE_SIZE = 128

HG_HEADS = 4
HG_DK = 128
HG_DV = 128
GLA_HEADS = 4
GLA_DK = 64
GLA_DV = 128
GLA_RANK = 16
GLA_GATE_NORM = 16.0
ML_HEADS = 4
ML_DK = 128
ML_DV = 128
N_BRANCH = 3
BRANCH_W = 512
D_FF = 2816
CHUNK = 64
EPS = 1e-6
NEG_BIG = -1e30

_SPLIT_SIZES = (
    HG_HEADS * HG_DK, HG_HEADS * HG_DK, HG_HEADS * HG_DV, HG_HEADS * HG_DV,
    GLA_HEADS * GLA_DK, GLA_HEADS * GLA_DK, GLA_HEADS * GLA_DV, GLA_HEADS * GLA_DV,
    GLA_RANK,
    ML_HEADS * ML_DK, ML_HEADS * ML_DK, ML_HEADS * ML_DV, ML_HEADS * ML_DV,
    ML_HEADS, ML_HEADS,
    N_BRANCH * D_MODEL,
)
D_IN = int(sum(_SPLIT_SIZES))
_SPLIT_IDX = [int(v) for v in np.cumsum(_SPLIT_SIZES)[:-1]]

kernel_name = "hybrid_hgrn2_gla_mlstm_macaron_step"

def rmsnorm(x, g):
    xf = x.astype(jnp.float32)
    y = xf * lax.rsqrt(jnp.mean(xf * xf, axis=-1, keepdims=True) + EPS)
    return (y * g.astype(jnp.float32)).astype(x.dtype)

def head_rmsnorm(o, g):
    return o * lax.rsqrt(jnp.mean(o * o, axis=-1, keepdims=True) + EPS) * g.astype(jnp.float32)

def split_heads(t, h):
    b, l, _ = t.shape
    return t.reshape(b, l, h, -1).transpose(0, 2, 1, 3)

def merge_heads(t):
    b, h, l, d = t.shape
    return t.transpose(0, 2, 1, 3).reshape(b, l, h * d)

def chunk_len(length):
    return CHUNK if length % CHUNK == 0 else length

def to_chunks(t, c):
    b, h, l = t.shape[:3]
    t = t.reshape((b, h, l // c, c) + t.shape[3:])
    return jnp.moveaxis(t, 2, 0)

def from_chunks(t):
    t = jnp.moveaxis(t, 0, 2)
    b, h, n, c = t.shape[:4]
    return t.reshape((b, h, n * c) + t.shape[4:])

def gated_linear_scan(q, k, v, logf, s0):
    c = chunk_len(q.shape[2])
    tri = jnp.tril(jnp.ones((c, c), dtype=bool))

    def step(s, inp):
        qc, kc, vc, gc = inp
        b = jnp.cumsum(gc, axis=2)
        diff = b[:, :, :, None, :] - b[:, :, None, :, :]
        decay = jnp.exp(jnp.where(tri[:, :, None], diff, NEG_BIG))
        att = jnp.einsum('bhtd,bhsd,bhtsd->bhts', qc, kc, decay)
        o = (jnp.einsum('bhts,bhsv->bhtv', att, vc)
             + jnp.einsum('bhtd,bhdv->bhtv', qc * jnp.exp(b), s))
        b_end = b[:, :, -1:, :]
        s_new = (jnp.exp(b_end[:, :, 0, :])[..., None] * s
                 + jnp.einsum('bhsd,bhsv->bhdv', kc * jnp.exp(b_end - b), vc))
        return s_new, o

    s_fin, o = lax.scan(step, s0, (to_chunks(q, c), to_chunks(k, c), to_chunks(v, c), to_chunks(logf, c)))
    return from_chunks(o), s_fin

def mlstm_scan(q, k, v, logi, logf, c0, n0, m0):
    c = chunk_len(q.shape[2])
    tri = jnp.tril(jnp.ones((c, c), dtype=bool))

    def step(carry, inp):
        cst, n, m = carry
        qc, kc, vc, ic, fc = inp
        b = jnp.cumsum(fc, axis=-1)
        log_d = jnp.where(tri, b[..., :, None] - b[..., None, :] + ic[..., None, :], NEG_BIG)
        inter = b + m[..., None]
        m_t = jnp.maximum(inter, jnp.max(log_d, axis=-1))
        d = jnp.exp(log_d - m_t[..., None])
        w_inter = jnp.exp(inter - m_t)
        qk = jnp.einsum('bhtd,bhsd->bhts', qc, kc) * d
        num = (jnp.einsum('bhts,bhsv->bhtv', qk, vc)
               + w_inter[..., None] * jnp.einsum('bhtd,bhdv->bhtv', qc, cst))
        den = jnp.sum(qk, axis=-1) + w_inter * jnp.einsum('bhtd,bhd->bht', qc, n)
        h = num / jnp.maximum(jnp.abs(den), jnp.exp(-m_t))[..., None]
        m_new = m_t[..., -1]
        w_s = jnp.exp(b[..., -1:] - b + ic - m_new[..., None])
        carry_decay = jnp.exp(b[..., -1] + m - m_new)
        c_new = carry_decay[..., None, None] * cst + jnp.einsum('bhs,bhsd,bhsv->bhdv', w_s, kc, vc)
        n_new = carry_decay[..., None] * n + jnp.einsum('bhs,bhsd->bhd', w_s, kc)
        return (c_new, n_new, m_new), h

    (c_f, n_f, m_f), h = lax.scan(
        step, (c0, n0, m0),
        (to_chunks(q, c), to_chunks(k, c), to_chunks(v, c), to_chunks(logi, c), to_chunks(logf, c)))
    return from_chunks(h), c_f, n_f, m_f

def swiglu_half(x, g, w_up, w_down):
    h = rmsnorm(x, g)
    gate, up = jnp.split(h @ w_up, 2, axis=-1)
    return x + 0.5 * ((jax.nn.silu(gate) * up) @ w_down)

def mixer(h, l, lb, p, st):
    dt = h.dtype
    f32 = lambda t: t.astype(jnp.float32)
    s_hg, s_gla, c_ml, n_ml, m_ml = [f32(s) for s in st]
    (hq, hf, hi, hg, gq, gk, gv, gg, glr, mq, mk, mv, mo, mi, mf, mg) = jnp.split(
        h @ p['w_in'][l], _SPLIT_IDX, axis=-1)

    zf = f32(hf)
    f_hg = lb + (1.0 - lb) * jax.nn.sigmoid(zf)
    log_f = jnp.log(f_hg)
    k_hg = (1.0 - lb) * jax.nn.sigmoid(-zf)
    o_hg, s_hg_new = gated_linear_scan(
        split_heads(jax.nn.silu(f32(hq)), HG_HEADS), split_heads(k_hg, HG_HEADS),
        split_heads(f32(hi), HG_HEADS), split_heads(log_f, HG_HEADS), s_hg)
    o_hg = merge_heads(head_rmsnorm(o_hg, p['hgrn_out_norm'][l])) * jax.nn.silu(f32(hg))

    log_a = jax.nn.log_sigmoid(f32(glr @ p['gla_w_gate_lr'][l]) + f32(p['gla_b_gate'][l])) / GLA_GATE_NORM
    o_gla, s_gla_new = gated_linear_scan(
        split_heads(f32(gq) * (GLA_DK ** -0.5), GLA_HEADS), split_heads(f32(gk), GLA_HEADS),
        split_heads(f32(gv), GLA_HEADS), split_heads(log_a, GLA_HEADS), s_gla)
    o_gla = merge_heads(head_rmsnorm(o_gla, p['gla_out_norm'][l])) * jax.nn.silu(f32(gg))

    logi = (f32(mi) + f32(p['mlstm_b_i'][l])).transpose(0, 2, 1)
    logfm = jax.nn.log_sigmoid(f32(mf) + f32(p['mlstm_b_f'][l])).transpose(0, 2, 1)
    h_ml, c_new, n_new, m_new = mlstm_scan(
        split_heads(f32(mq), ML_HEADS), split_heads(f32(mk) * (ML_DK ** -0.5), ML_HEADS),
        split_heads(f32(mv), ML_HEADS), logi, logfm, c_ml, n_ml, m_ml)
    o_ml = merge_heads(head_rmsnorm(h_ml, p['mlstm_out_norm'][l])) * jax.nn.sigmoid(f32(mo))

    b_, l_, _ = h.shape
    branches = jnp.stack([o_hg, o_gla, o_ml], axis=2).astype(dt)
    proj = jnp.einsum('blcw,cwd->blcd', branches, p['w_branch'][l])
    gates = jax.nn.sigmoid(mg).reshape(b_, l_, N_BRANCH, D_MODEL)
    merged = jnp.einsum('blcd,blcd->bld', gates, proj)
    y = merged @ p['w_out'][l]
    return y, (s_hg_new, s_gla_new, c_new, n_new, m_new)

def trunk(x, states, p):
    lb_soft = jax.nn.softmax(p['hgrn_lb_raw'].astype(jnp.float32), axis=0)
    lb_all = jnp.cumsum(lb_soft, axis=0) - lb_soft[0]
    outs = ([], [], [], [], [])
    for l in range(DEPTH):
        x = swiglu_half(x, p['ffn1_norm'][l], p['ffn1_w_up'][l], p['ffn1_w_down'][l])
        y, st = mixer(rmsnorm(x, p['mix_norm'][l]), l, lb_all[l], p, tuple(s[l] for s in states))
        x = x + y
        x = swiglu_half(x, p['ffn2_norm'][l], p['ffn2_w_up'][l], p['ffn2_w_down'][l])
        for acc, s in zip(outs, st):
            acc.append(s)
    return rmsnorm(x, p['final_norm']), tuple(jnp.stack(a) for a in outs)

def setup_inputs(seed: int = 0) -> dict:
    key = jax.random.key(seed)
    ks = jax.random.split(key, 32)
    nrm = lambda k, shape, scale: jax.random.normal(k, shape, jnp.float32) * scale
    gain = lambda k, shape: 1.0 + nrm(k, shape, 0.02)
    hd = (DEPTH, DEC_BATCH)
    return {
        "x_prompt": nrm(ks[0], (BATCH, SEQ, D_MODEL), 1.0),
        "x_sample": nrm(ks[1], (DEC_BATCH, DEC_SEQ, D_MODEL), 1.0),
        "state_hgrn": nrm(ks[2], hd + (HG_HEADS, HG_DK, HG_DV), 0.5),
        "state_gla": nrm(ks[3], hd + (GLA_HEADS, GLA_DK, GLA_DV), 1.0),
        "state_mlstm_C": nrm(ks[4], hd + (ML_HEADS, ML_DK, ML_DV), 0.5),
        "state_mlstm_n": nrm(ks[5], hd + (ML_HEADS, ML_DK), 0.5),
        "state_mlstm_m": nrm(ks[6], hd + (ML_HEADS,), 1.0),
        "ffn1_norm": gain(ks[7], (DEPTH, D_MODEL)),
        "ffn1_w_up": nrm(ks[8], (DEPTH, D_MODEL, 2 * D_FF), D_MODEL ** -0.5),
        "ffn1_w_down": nrm(ks[9], (DEPTH, D_FF, D_MODEL), D_FF ** -0.5),
        "mix_norm": gain(ks[10], (DEPTH, D_MODEL)),
        "w_in": nrm(ks[11], (DEPTH, D_MODEL, D_IN), D_MODEL ** -0.5),
        "hgrn_lb_raw": nrm(ks[12], (DEPTH, HG_HEADS * HG_DK), 0.1),
        "hgrn_out_norm": gain(ks[13], (DEPTH, HG_DV)),
        "gla_w_gate_lr": nrm(ks[14], (DEPTH, GLA_RANK, GLA_HEADS * GLA_DK), GLA_RANK ** -0.5),
        "gla_b_gate": nrm(ks[15], (DEPTH, GLA_HEADS * GLA_DK), 0.1),
        "gla_out_norm": gain(ks[16], (DEPTH, GLA_DV)),
        "mlstm_b_i": nrm(ks[17], (DEPTH, ML_HEADS), 0.1),
        "mlstm_b_f": jnp.linspace(3.0, 6.0, ML_HEADS, dtype=jnp.float32)[None, :] + nrm(ks[18], (DEPTH, ML_HEADS), 0.1),
        "mlstm_out_norm": gain(ks[19], (DEPTH, ML_DV)),
        "w_branch": nrm(ks[20], (DEPTH, N_BRANCH, BRANCH_W, D_MODEL), BRANCH_W ** -0.5),
        "w_out": nrm(ks[21], (DEPTH, D_MODEL, D_MODEL), D_MODEL ** -0.5),
        "ffn2_norm": gain(ks[22], (DEPTH, D_MODEL)),
        "ffn2_w_up": nrm(ks[23], (DEPTH, D_MODEL, 2 * D_FF), D_MODEL ** -0.5),
        "ffn2_w_down": nrm(ks[24], (DEPTH, D_FF, D_MODEL), D_FF ** -0.5),
        "final_norm": gain(ks[25], (D_MODEL,)),
    }

def reference(x_prompt, x_sample, state_hgrn, state_gla, state_mlstm_C, state_mlstm_n, state_mlstm_m,
              ffn1_norm, ffn1_w_up, ffn1_w_down, mix_norm, w_in, hgrn_lb_raw, hgrn_out_norm,
              gla_w_gate_lr, gla_b_gate, gla_out_norm, mlstm_b_i, mlstm_b_f, mlstm_out_norm,
              w_branch, w_out, ffn2_norm, ffn2_w_up, ffn2_w_down, final_norm):
    p = dict(ffn1_norm=ffn1_norm, ffn1_w_up=ffn1_w_up, ffn1_w_down=ffn1_w_down, mix_norm=mix_norm,
             w_in=w_in, hgrn_lb_raw=hgrn_lb_raw, hgrn_out_norm=hgrn_out_norm,
             gla_w_gate_lr=gla_w_gate_lr, gla_b_gate=gla_b_gate, gla_out_norm=gla_out_norm,
             mlstm_b_i=mlstm_b_i, mlstm_b_f=mlstm_b_f, mlstm_out_norm=mlstm_out_norm,
             w_branch=w_branch, w_out=w_out, ffn2_norm=ffn2_norm, ffn2_w_up=ffn2_w_up,
             ffn2_w_down=ffn2_w_down, final_norm=final_norm)
    bp = (DEPTH, BATCH)
    zero_states = (
        jnp.zeros(bp + (HG_HEADS, HG_DK, HG_DV), jnp.float32),
        jnp.zeros(bp + (GLA_HEADS, GLA_DK, GLA_DV), jnp.float32),
        jnp.zeros(bp + (ML_HEADS, ML_DK, ML_DV), jnp.float32),
        jnp.zeros(bp + (ML_HEADS, ML_DK), jnp.float32),
        jnp.zeros(bp + (ML_HEADS,), jnp.float32),
    )
    y_prompt, ps = trunk(x_prompt, zero_states, p)
    y_sample, ss = trunk(x_sample, (state_hgrn, state_gla, state_mlstm_C, state_mlstm_n, state_mlstm_m), p)
    return (y_prompt, y_sample, ps[0], ps[1], ps[2], ps[3], ps[4], ss[0], ss[1], ss[2], ss[3], ss[4])


_drawn_inputs = setup_inputs


def setup_inputs(seed=0):
    import zlib

    import numpy as np

    out = dict(_drawn_inputs(seed))
    spreads = {}
    factors = {'ffn1_norm': 2.777,
     'hgrn_out_norm': 17.89,
     'gla_out_norm': 20.216,
     'mlstm_out_norm': 23.489,
     'ffn2_norm': 5.245,
     'final_norm': 7.84}
    for name, (base, spread) in spreads.items():
        noise = np.random.default_rng([zlib.crc32(name.encode()), seed]).standard_normal(out[name].shape)
        drawn = base * np.exp(spread * noise) if base else spread * noise
        out[name] = jnp.asarray(drawn.astype(out[name].dtype))
    for name, factor in factors.items():
        out[name] = (out[name] * factor).astype(out[name].dtype)
    return out
```

```python
import numpy as np
from contextlib import ExitStack

import concourse.bass as bass
from concourse import mybir

F32, F32R, U8 = mybir.dt.float32, mybir.dt.float32r, mybir.dt.uint8
ALU = mybir.AluOpType
ACT = mybir.ActivationFunctionType

P = 128
D_MODEL, D_FF, DEPTH = 1024, 2816, 2
SEQ, DEC_B, DEC_T = 512, 8, 4
SMP = DEC_B * DEC_T
TOK = SEQ + SMP
HALF = TOK // 2
KT = D_MODEL // P
HEADS, CH = 4, 128
NCH = SEQ // CH
LEVELS = 7
S_LEVELS = 2
EPS = 1e-6

FF_BLOCK = 8
FF_TILES = D_FF // P
FF_LAST = FF_TILES - 2 * FF_BLOCK
FFN_TILES = 2 * FF_TILES + 3 * KT

HQ, HF, HI, HG, SMALL, GQ, GK, GV, GG = 0, 4, 8, 12, 16, 17, 19, 21, 25
MIX_TILES = 102
MIX_PIECES = 92
MIX_T0 = MIX_P0 = FFN_TILES
FFN2_T0, FFN2_P0 = MIX_T0 + MIX_TILES, MIX_P0 + MIX_PIECES
TILES, PIECES = FFN2_T0 + FFN_TILES, FFN2_P0 + FFN_TILES
G0, B0, ML, G1, B1, G2, B2, WO = (29, 29), (37, 37), (45, 41), (61, 57), (69, 65), (77, 69), (85, 77), (93, 81)
ONE = 1
RING = 2
RAW = 2
assert TILES % 2 == 0 and PIECES % 4 == 0

PG = {"ffn1": 0, "mix": 8, "ffn2": 16}
P_HN, P_BG, P_BI, P_BF, P_LR = 24, 27, 29, 30, 31
NPAR = P_LR + 256
C_ID, C_DIAG, C_NEG = 0, 128, 256
C_NEGS = C_NEG + 128
C_SEL = C_NEGS + 32
C_BM = C_SEL + 512
NCONST = C_BM + 8

def scan_steps(br):
    if br < 2:
        s = [(("v", br, 0), 2), (("v", br, 1), 2), (("d", br, 0), 2), (("d", br, 1), 4)]
        s += [(("lv", br, l), 6 if l <= S_LEVELS else 5) for l in range(1, LEVELS + 1)]
        s += [(("k", br, 0), 3), (("k", br, 1), 1), (("u", br, 0), 7)]
    else:
        s = [(("v", br, 0), 2), (("v", br, 1), 2)] + [(("a", br, h), 6) for h in range(HEADS)]
        s += [(("k", br, 0), 7), (("k", br, 1), 2), (("u", br, 0), 7), (("un", br, 0), 5), (("ns", br, 0), 1)]
    for h in range(HEADS):
        s += [(("m", br, h), 3)] if br == 2 else []
        s += [(("o", br, h), 8 if br == 2 else 3), (("z", br, h), 3), (("n", br, h), 6)]
    return s


def weave(tiles, steps, keep=2):
    out, n, spent = [], 0, 0
    total = sum(w for _, w in steps)
    for s, w in steps:
        out.append(s)
        spent += w
        upto = spent * (len(tiles) - keep) // total
        out += tiles[n:upto]
        n = upto
    return out + tiles[n:]


def mixer_order():
    def group(t0, t1):
        return [("tile", t, 0) for t in range(t0, t1)]

    def branch(b):
        return [("branch", b, m) for m in range(KT)]

    return (group(0, SMALL + 1) + [("rows", 0, 0)] + group(GQ, GV) + [("cols", 0, 0)]
            + weave(group(GV, G0[0]) + group(G0[0], B0[0]), scan_steps(0))
            + weave(branch(0) + group(ML[0], G1[0]), scan_steps(1))
            + weave(group(G1[0], B1[0]) + branch(1) + group(G2[0], B2[0]), scan_steps(2), 4)
            + branch(2) + [("out", 0, 0)])


ORDER = mixer_order()
STEP_NO = {s: i for i, s in enumerate([s for s in ORDER if s[0] not in ("tile", "branch", "out")])}
NSTEPS = len(STEP_NO)


def piece_of(t):
    for t0, p0 in (WO, G2, G1, ML):
        if t >= t0:
            return p0 + t - t0
    return t


class Chain:

    def __init__(self, eng, sem):
        self.eng, self.sem, self.base, self.n = eng, sem, ONE, 0

    def did(self, ins):
        ins.then_inc(self.sem, 1)
        self.n += 1

    def sync(self):
        self.eng.wait_ge(self.sem, self.base + self.n)

    def link(self, ins):
        self.did(ins)
        self.sync()

    def loop(self, reg, per):
        outer = Chain(self.eng, self.sem)
        outer.base, outer.n = self.base, self.n
        self.base, self.n = self.base + self.n + reg * per, 0
        return outer

    def end(self, outer, per, times):
        self.sync()
        assert self.n <= per, self.n
        if self.n < per:
            self.eng.sem_inc(self.sem, per - self.n)
        self.base, self.n = outer.base, outer.n + per * times


def build(nc, wst, xT, par_d, lb_d, const_d, lvm_d, fg_d, st_h, st_g, st_c, st_n, st_m,
          yT, p_h, p_g, p_c, p_n, s_h, s_g, s_c, s_n, s_m, x_keep):
    ctx = ExitStack()
    with ctx:
        top = [(nc.sbuf_base + 31) // 32 * 32]

        def sb(name, shape, dt=F32, at=None):
            size = 1 if dt == U8 else 4
            for d in shape[1:]:
                size *= d
            if at is None:
                at = top[0]
                top[0] += (size + 31) // 32 * 32
            return nc.alloc_sbuf_tensor_at(name, shape, dt, offset=at), at

        X, _ = sb("X", [P, KT, TOK])
        Hh, _ = sb("Hh", [P, KT, TOK], F32R)
        Hl, _ = sb("Hl", [P, KT, TOK], F32R)
        raw, _ = sb("raw", [P, RAW, 1024])
        Wh, _ = sb("Wh", [P, RING, 1024], F32R)
        Wl, _ = sb("Wl", [P, RING, 1024], F32R)
        const, _ = sb("const", [P, NCONST])
        ones, _ = sb("ones", [P, P])
        par, _ = sb("par", [P, NPAR])
        parL, _ = sb("parL", [P, DEPTH, 31])
        lvm, _ = sb("lvm", [P, LEVELS * P], U8)
        lbs, _ = sb("lbs", [P, DEPTH, 4])
        lbc, _ = sb("lbc", [P, 8])
        lbt, _ = sb("lbt", [P, 24])
        fg, _ = sb("fg", [P, KT])
        epsc, _ = sb("epsc", [P, 1])
        tmp, tmp_at = sb("tmp", [P, 6, TOK])
        vblk, _ = sb("vblk", [SMP, 1024], at=tmp_at + 3 * TOK * 4)
        dec, _ = sb("dec", [P, HEADS, NCH])
        decs, _ = sb("decs", [P, HEADS, DEC_B])
        wrow, _ = sb("wrow", [P, TOK])
        colG, _ = sb("colG", [P, 16])
        colW, _ = sb("colW", [P, 16])
        colS, _ = sb("colS", [SMP, 8])
        nst, nst_at = sb("nst", [SMP + HEADS, P])
        nS, _ = sb("nS", [P, SMP])
        nP, _ = sb("nP", [P, HEADS, NCH])
        nO, _ = sb("nO", [P, SMP + HEADS])
        nOt, _ = sb("nOt", [SMP + HEADS, P], at=nst_at)
        m0, _ = sb("m0", [HEADS, DEC_B])
        mO, _ = sb("mO", [HEADS, 1 + DEC_B])
        mch, _ = sb("mch", [HEADS, 1 + NCH])
        arena = top[0]
        setA, a_at = sb("setA", [P, 16, TOK])
        setB, b_at = sb("setB", [P, 16, TOK])
        kbuf, _ = sb("kbuf", [P, 4, TOK])
        att, att_at = sb("att", [P, 4, TOK])
        vts, _ = sb("vts", [SMP, 4, P])
        kts, _ = sb("kts", [SMP, 4, P])
        sst, _ = sb("sst", [P, DEC_B, P])
        gates, gates_at = sb("gates", [P, KT, TOK])
        rows, _ = sb("rows", [P, 6, TOK], at=gates_at)
        glr, _ = sb("glr", [16, TOK], at=gates_at + 6 * TOK * 4)
        oh = [sb("ohA", [P, 4, TOK], F32R, a_at)[0], sb("ohB", [P, 4, TOK], F32R, b_at)[0]]
        olo = [sb("olA", [P, 4, TOK], F32R, a_at + 8 * TOK * 4)[0], sb("olB", [P, 4, TOK], F32R, b_at + 8 * TOK * 4)[0]]
        Ah, f1 = sb("Ah", [P, FF_BLOCK, TOK], F32R, arena)
        Al, f2 = sb("Al", [P, FF_BLOCK, TOK], F32R, arena + FF_BLOCK * TOK * 4)

        SETS = [setA, setB, setA]
        R0 = [s[:, 0:4, :] for s in SETS]
        R1 = [s[:, 4:8, :] for s in SETS]
        R2 = [s[:, 8:12, :] for s in SETS]
        R3 = [s[:, 12:16, :] for s in SETS]
        KB = [kbuf[:, :, :], R1[1][:, 2:4, :], R1[2]]
        KTOK = [R1[0], R1[1][:, 0:2, :], kbuf[:, :, :]]
        OB = [R1[0], kbuf[:, :, :], kbuf[:, :, :]]
        OH = [oh[0], oh[1], oh[0]]
        OL = [olo[0], olo[1], olo[0]]

        dps = [ctx.enter_context(nc.psum_tensor(f"dense{i}", [P, 2, 512], F32)) for i in range(2)]
        SA = ctx.enter_context(nc.psum_tensor("SA", [P, 2, 512], F32))
        SB = ctx.enter_context(nc.psum_tensor("SB", [P, 2, 512], F32))

        def sem(name):
            return ctx.enter_context(nc.semaphore(name))

        raw_in = [sem(f"raw_in{i}") for i in range(RAW)]
        raw_free = sem("raw_free")
        w_ready = sem("w_ready")
        w_used = sem("w_used")
        tile_done = sem("tile_done")
        slot_free = [sem(f"slot_free{i}") for i in range(2)]
        consts_in = sem("consts_in")
        x_in = sem("x_in")
        dlink, alink, glink = sem("dlink"), sem("alink"), sem("glink")
        const_ready = sem("const_ready")
        ssq_ready, rms_sum, rs_ready = sem("ssq_ready"), sem("rms_sum"), sem("rs_ready")
        norm_h, norm_hi, norm_lo = sem("norm_h"), sem("norm_hi"), sem("norm_lo")
        ffn_hi, ffn_lo = sem("ffn_hi"), sem("ffn_lo")
        sig_done = sem("sig_done")
        x_read = sem("x_read")
        la_1, la_2, la_3 = sem("la_1"), sem("la_2"), sem("la_3")
        lr_used = sem("lr_used")
        pe_step, dve_step, act_step = sem("pe_step"), sem("dve_step"), sem("act_step")
        step_began = sem("step_began")
        split_began = sem("split_began")
        dve_began = sem("dve_began")
        row_x = sem("row_x")
        row_y = sem("row_y")
        m_in = sem("m_in")
        st_in, st_out = sem("st_in"), sem("st_out")
        st_mem = sem("st_mem")
        d_exp, e_exp, d_abs = sem("d_exp"), sem("e_exp"), sem("d_abs")
        h_rs, h_of, h_hi, h_lo = sem("h_rs"), sem("h_of"), sem("h_hi"), sem("h_lo")
        br_sig = sem("br_sig")
        mg_f, mg_hi, mg_lo = sem("mg_f"), sem("mg_hi"), sem("mg_lo")
        x_back = sem("x_back")
        y_ready, y_out = sem("y_ready"), sem("y_out")
        out_sem = sem("out_sem")

        ident = const[:, C_ID:C_ID + 128]
        diag = const[:, C_DIAG:C_DIAG + 128]

        def mask(l):
            return lvm[:, (l - 1) * P:l * P]

        def halves(ap):
            return ap.rearrange("p (a b) -> p a b", a=2)

        def f32(ap):
            return ap.bitcast(F32)

        def kt(br, h):
            return h // 2 if br == 1 else h

        def st_no(br, h):
            return h if br == 0 else 4 + h // 2 if br == 1 else 6 + h

        block = ctx.enter_context(nc.Block())

        @block.sync
        def _(sp):
            sp.sem_inc(raw_free, RAW)
            with sp.Fori(0, DEPTH * PIECES // 4) as it:
                for j in range(4):
                    sp.wait_ge(raw_free, it * 4 + (j + 1))
                    sp.dma_start(raw[:, j % RAW, :], wst[it * 4 + j, :, :]).then_inc(raw_in[j % RAW], 16)

        @block.gpsimd
        def _(pool):
            pool.sem_inc(w_used, RING - 1)
            with pool.Fori(0, DEPTH * PIECES // 4) as it:
                for j in range(4):
                    s, r = j % RING, j % RAW
                    pool.wait_ge(raw_in[r], it * (64 // RAW) + 16 * (j // RAW + 1))
                    pool.wait_ge(w_used, it * 4 + (j + 1))
                    pool.sem_inc(split_began, 1)
                    pool.tensor_scalar(Wh[:, s, :], raw[:, r, :], 1.0, 0.0, ALU.mult, ALU.add).then_inc(glink, 1)
                    pool.wait_ge(glink, it * 8 + (2 * j + 1))
                    pool.tensor_tensor(Wl[:, s, :], raw[:, r, :], f32(Wh[:, s, :]),
                                       ALU.subtract).then_inc(glink, 1)
                    pool.wait_ge(glink, it * 8 + (2 * j + 2))
                    pool.sem_inc(w_ready, 1)
                    pool.sem_inc(raw_free, 1)

        @block.tensor
        def _(pe):
            def dense(p, t, ring, slot, use, hi, lo, k0, nk, first=None):
                pe.wait_ge(w_ready, p + 1)
                pe.wait_ge(slot_free[slot], ONE + use)
                for k in range(nk):
                    if first is not None:
                        pe.wait_ge(first[0], first[1] + (k + 1))
                    w0 = (k0 + k) * 128
                    for n, (w, x) in enumerate(((Wh, hi), (Wh, lo), (Wl, hi))):
                        for a in range(2):
                            mm = pe.matmul(dps[slot][:, a, 0:HALF], w[:, ring, w0:w0 + 128],
                                           x[:, k, a * HALF:(a + 1) * HALF],
                                           start=(k == 0 and n == 0), stop=(k == nk - 1 and n == 2))
                    if k == 0 and k0 == 0:
                        pe.wait_ge(tile_done, ONE + t)
                        pe.sem_inc(w_used, 1)
                mm.then_inc(tile_done, 1)

            def rms(n):
                pe.wait_ge(ssq_ready, n + 1)
                for a in range(2):
                    mm = pe.matmul(SB[:, a, 0:HALF], ones[:, :], tmp[:, 3, a * HALF:(a + 1) * HALF],
                                   start=True, stop=True)
                mm.then_inc(rms_sum, 1)

            def ffn(L, t0, p0, norm_no, which):
                rms(norm_no)

                for b, nf in enumerate((FF_BLOCK, FF_BLOCK, FF_LAST)):
                    off = b * 24
                    with pe.Fori(0, nf // 2) as i:
                        for j in range(4):
                            u = L * (TILES // 2) + (t0 + off) // 2 + i * 2 + j // 2
                            dense(L * PIECES + (p0 + off + j) + i * 4, L * TILES + (t0 + off + j) + i * 4, j % RING, j % 2, u, Hh, Hl, 0, KT,
                                  (norm_lo, norm_no * KT) if b == 0 and j == 0 else None)
                    hidden = L * (2 * FF_TILES) + (which * FF_TILES + b * FF_BLOCK)
                    with pe.Fori(0, 2) as i:
                        for j in range(4):
                            u = L * (TILES // 2) + (t0 + off + 2 * nf) // 2 + i * 2 + j // 2
                            dense(L * PIECES + (p0 + off + 2 * nf + j) + i * 4,
                                  L * TILES + (t0 + off + 2 * nf + j) + i * 4, j % RING, j % 2, u,
                                  Ah, Al, 0, nf, (ffn_lo, hidden) if j == 0 else None)

            def tile(L, t, hi, lo, nk=KT, p=None, k0=0, first=None):
                g = MIX_T0 + t
                p = piece_of(t) if p is None else p
                dense(L * PIECES + (MIX_P0 + p), L * TILES + g, (MIX_P0 + p) % RING, g % 2, L * (TILES // 2) + g // 2,
                      hi, lo, k0, nk, first)

            def tpose(out, in_, idn):
                return pe.transpose(out, in_, idn)

            def step(L, s):
                kind, br, h = s
                no = L * NSTEPS + STEP_NO[s]
                pe.wait_ge(dve_step, ONE + no)
                pe.wait_ge(act_step, ONE + no)
                pe.sem_inc(step_began, 1)
                mm = None
                Q, K, V = R0[br], KB[br], R2[br]
                Tk, att_ = KTOK[br], att
                if kind == "rows":
                    pe.wait_ge(lr_used, L * 2 + 1)
                    for i in range(2):
                        for a in range(2):
                            bank = (SA, SB)[i]
                            mm = pe.matmul(bank[:, a, 0:HALF], par[0:16, P_LR + i * 128:P_LR + (i + 1) * 128],
                                           glr[:, a * HALF:(a + 1) * HALF], start=True, stop=True)
                elif kind == "cols":
                    for r, c0 in ((4, 0), (5, 32)):
                        for c in range(NCH):
                            tpose(SA[:, 0, c0 + c * 4:c0 + c * 4 + 4], rows[0:4, r, c * CH:(c + 1) * CH],
                                  ident[0:4, 0:4])
                        tpose(SA[0:SMP, 1, c0:c0 + 4], rows[0:4, r, SEQ:TOK], ident[0:4, 0:4])
                    pe.wait_ge(m_in, L * 32 + 32)
                    pe.sem_inc(step_began, 1)
                    mm = tpose(SB[:, 0, 0:SMP], nst[0:SMP, :], ident[0:SMP, 0:SMP])
                elif kind == "v":
                    for i in range(2):
                        for c in range(NCH):
                            tpose(SA[:, i, c * CH:(c + 1) * CH], V[:, 2 * h + i, c * CH:(c + 1) * CH], ident)
                        mm = tpose(SB[0:SMP, 0, i * P:(i + 1) * P], V[:, 2 * h + i, SEQ:TOK], ident)
                elif kind == "d":
                    for i in range(2):
                        hh = 2 * h + i
                        for c in range(NCH):
                            cs = slice(c * CH, (c + 1) * CH)
                            mm = pe.matmul(SA[:, i, cs], K[:, kt(br, hh), cs], Q[:, hh, cs], start=True, stop=True)
                    if h == 0:
                        for hh in range(HEADS):
                            mm = pe.matmul(SB[0:SMP, 0, hh * SMP:(hh + 1) * SMP], K[:, kt(br, hh), SEQ:TOK],
                                           Q[:, hh, SEQ:TOK], start=True, stop=True)
                elif kind == "lv":
                    bs, hf = 1 << h, 1 << (h - 1)
                    for hh in range(HEADS):
                        for c in range(NCH):
                            col = (hh % 2) * 256 + c * 64
                            if hf >= 32:
                                for s0 in range(0, CH, bs):
                                    o0 = col + s0 // bs * hf
                                    mm = pe.matmul(SA[s0:s0 + hf, hh // 2, o0:o0 + hf],
                                                   K[:, kt(br, hh), c * CH + s0:c * CH + s0 + hf],
                                                   Q[:, hh, c * CH + s0 + hf:c * CH + s0 + bs],
                                                   start=True, stop=True)
                                continue
                            q = Q[:, hh, c * CH:(c + 1) * CH].rearrange("p (n b) -> p n b", b=bs)[:, :, hf:bs]
                            mm = pe.matmul(SA[:, hh // 2, col:col + 64], K[:, kt(br, hh), c * CH:(c + 1) * CH],
                                           q, start=True, stop=True)
                    if h <= S_LEVELS:
                        for hh in range(HEADS):
                            mm = pe.matmul(SB[0:SMP, 0, hh * SMP:(hh + 1) * SMP], K[:, kt(br, hh), SEQ:TOK],
                                           Q[:, hh, SEQ:TOK], start=True, stop=True)
                elif kind == "a":
                    for c in range(NCH):
                        cs = slice(c * CH, (c + 1) * CH)
                        pe.matmul(SA[:, 1, cs], K[:, h, cs], Q[:, h, cs], start=True, stop=True)
                    pe.matmul(SB[0:SMP, 0, 32:64], K[:, h, SEQ:TOK], Q[:, h, SEQ:TOK], start=True, stop=True)
                    s0, s1 = sel(0, h), sel(1, h)
                    pe.matmul(SA[:, 0, :], s0, wrow[0:4, 0:SEQ], start=True, stop=True)
                    pe.matmul(SB[0:SMP, 0, 0:32], s0[:, 0:SMP], wrow[0:4, SEQ:TOK], start=True, stop=True)
                    pe.matmul(SB[:, 1, :], s1, wrow[32:36, 0:SEQ], start=True, stop=True)
                    mm = pe.matmul(SB[:, 0, 64:96], s1, wrow[32:36, SEQ:TOK], start=True, stop=True)
                elif kind == "k":
                    nt = 2 if br == 1 else 4
                    for i in range(nt):
                        if h == 0:
                            for c in range(NCH):
                                mm = tpose((SA, SB)[i // 2][:, i % 2, c * CH:(c + 1) * CH],
                                           K[:, i, c * CH:(c + 1) * CH], ident)
                        else:
                            mm = tpose(SA[0:SMP, 0, i * P:(i + 1) * P], K[:, i, SEQ:TOK], ident)
                elif kind == "u":
                    for hh in range(HEADS):
                        for c in range(NCH):
                            cs = slice(c * CH, (c + 1) * CH)
                            if br == 1:
                                e = 64 * (hh % 2)
                                mm = pe.matmul(SA[e:e + 64, hh // 2, cs], Tk[:, hh // 2, c * CH + e:c * CH + e + 64],
                                               V[:, hh, cs], start=True, stop=True)
                            else:
                                mm = pe.matmul((SA, SB)[hh // 2][:, hh % 2, cs], Tk[:, hh, cs], V[:, hh, cs],
                                               start=True, stop=True)
                elif kind == "un":
                    for hh in range(HEADS):
                        for c in range(NCH):
                            pe.matmul(SA[:, 0, hh * 4 + c:hh * 4 + c + 1], Tk[:, hh, c * CH:(c + 1) * CH],
                                      ones[:, 0:1], start=True, stop=True)
                        mm = pe.matmul(SA[:, 0, 64 + hh * 8:72 + hh * 8], kts[:, hh, :],
                                       const[0:SMP, C_BM:C_BM + 8], start=True, stop=True)
                elif kind == "ns":
                    mm = tpose(SA[0:SMP + HEADS, 0, 0:P], nO[:, :], ident)
                elif kind == "m":
                    pe.matmul(SA[:, 0, :], sel(2, h), wrow[64:68, 0:SEQ], start=True, stop=True)
                    mm = pe.matmul(SA[:, 1, 0:SMP], sel(2, h), wrow[64:68, SEQ:TOK], start=True, stop=True)
                elif kind == "o":
                    pe.wait_ge(st_in, L * 160 + 16 * (st_no(br, h) + 1))
                    for c in range(NCH):
                        cs = slice(c * CH, (c + 1) * CH)
                        pe.matmul(SA[:, 0, cs], V[:, h, cs], att[:, h, cs], start=True, stop=(c == 0))
                        if c:
                            ps = slice((c - 1) * CH, c * CH)
                            pe.matmul(SA[:, 0, cs], K[:, kt(br, h), ps], Q[:, h, cs], start=False, stop=True)
                    if br == 2:
                        pe.matmul(SB[:, 0, 0:CH], ones[:, :], att[:, h, 0:CH], start=True, stop=True)
                        pe.matmul(SB[:, 0, CH:SEQ], ones[:, :], att[:, h, CH:SEQ], start=True, stop=False)
                        pe.matmul(SB[:, 0, CH:SEQ], ones[:, :], tmp[:, 5, CH:SEQ], start=False, stop=True)
                        pe.matmul(SB[:, 1, 0:SMP], ones[0:SMP, :], att[0:SMP, h, SEQ:TOK], start=True, stop=False)
                        pe.matmul(SB[:, 1, 0:SMP], ones[:, :], tmp[:, 5, SEQ:TOK], start=False, stop=True)
                    pe.matmul(SA[:, 1, 0:SMP], vts[:, h, :], att[0:SMP, h, SEQ:TOK], start=True, stop=False,
                              skip_group_check=True)
                    for b in range(DEC_B):
                        mm = pe.matmul(SA[:, 1, b * DEC_T:(b + 1) * DEC_T], sst[:, b, :],
                                       Q[:, h, SEQ + b * DEC_T:SEQ + (b + 1) * DEC_T],
                                       start=False, stop=(b == DEC_B - 1), skip_group_check=True)
                elif kind == "z":
                    for i in range(2):
                        if br == 1:
                            e = 64 * (h % 2)
                            mm = pe.matmul(SB[e:e + 64, i, :], kts[:, h // 2, e:e + 64],
                                           vblk[:, i * 512:(i + 1) * 512], start=True, stop=True)
                        else:
                            mm = pe.matmul(SB[:, i, :], kts[:, h, :], vblk[:, i * 512:(i + 1) * 512],
                                           start=True, stop=True)
                elif kind == "n":
                    for a in range(2):
                        mm = pe.matmul(SB[:, a, 0:HALF], ones[:, :], tmp[:, 2, a * HALF:(a + 1) * HALF],
                                       start=True, stop=True)
                mm.then_inc(pe_step, 1)

            def sel(q, h):
                return const[32 * q:32 * q + 4, C_SEL + h * 128:C_SEL + (h + 1) * 128]

            pe.sem_inc(tile_done, ONE)
            pe.sem_inc(pe_step, ONE)
            pe.wait_ge(const_ready, 2)
            with pe.Fori(0, DEPTH) as L:
                ffn(L, 0, 0, L * 3, 0)
                rms(L * 3 + 1)
                for s in ORDER:
                    what, n, m = s
                    if what == "tile":
                        tile(L, n, Hh, Hl, first=(norm_lo, (L * 3 + 1) * KT) if n == 0 else None)
                    elif what == "branch":
                        t0, p0 = (B0, B1, B2)[n]
                        tile(L, t0 + m, OH[n], OL[n], 4, p0 + m // 2, 4 * (m % 2),
                             first=(h_lo, L * 12 + n * 4) if m == 0 else None)
                    elif what == "out":
                        pass
                    else:
                        step(L, s)
                for m in range(KT):
                    tile(L, WO[0] + m, Hh, Hl, first=(mg_lo, L * KT) if m == 0 else None)
                pe.wait_ge(tile_done, ONE + L * TILES + (FFN2_T0 - 1))
                pe.sem_inc(w_used, 3)
                pe.sem_inc(tile_done, 1)
                ffn(L, FFN2_T0, FFN2_P0, L * 3 + 2, 1)
            rms(3 * DEPTH)

        @block.scalar
        def _(act):
            ch = Chain(act, alink)
            act.sem_inc(alink, ONE)
            act.sem_inc(act_step, ONE)
            act.sem_inc(slot_free[0], ONE)

            def act_norm(n, final=False):
                act.wait_ge(rms_sum, n + 1)
                ch.sync()
                ch.link(act.activation(halves(tmp[:, 2, :]), SB[:, :, 0:HALF], ACT.Ln, bias=epsc[:, :],
                                       scale=1.0 / D_MODEL))
                act.activation(tmp[:, 2, :], tmp[:, 2, :], ACT.Exp, scale=-0.5).then_inc(rs_ready, 1)
                if final:
                    return
                for k in range(KT):
                    act.wait_ge(norm_h, n * KT + (k + 1))
                    act.activation(Hh[:, k, :], tmp[:, k % 2, :], ACT.Copy).then_inc(norm_hi, 1)

            def ffn(L, t0, norm_no, which):
                act_norm(norm_no)
                for b, nf in enumerate((FF_BLOCK, FF_BLOCK, FF_LAST)):
                    off = b * 24
                    with act.Fori(0, nf // 2) as i:
                        for j in range(2):
                            f = L * (2 * FF_TILES) + (which * FF_TILES + b * FF_BLOCK + j) + i * 2
                            use = L * (TILES // 2) + ((t0 + off) // 2 + j + 1) + i * 2
                            act.wait_ge(tile_done, ONE + L * TILES + (t0 + off + 2 * j + 1) + i * 4)
                            act.activation(halves(tmp[:, 4 + j, :]), dps[0][:, :, 0:HALF],
                                           ACT.Silu).then_inc(slot_free[0], 1)
                            act.wait_ge(slot_free[1], ONE + use)
                            act.activation(Ah[:, bass.ds(i * 2 + j, 1), :], tmp[:, j:j + 1, :],
                                           ACT.Copy).then_inc(ffn_hi, 1)

            def tile_wait(L, t):
                act.wait_ge(tile_done, ONE + L * TILES + (MIX_T0 + t + 1))

            def tile(L, t):
                slot = (MIX_T0 + t) % 2
                ps = dps[slot][:, :, 0:HALF]
                free = slot_free[slot]
                if t in range(HQ, HF) or t in range(HG, SMALL) or t in range(GG, G0[0]):
                    tile_wait(L, t)
                    act.wait_ge(free, ONE + L * (TILES // 2) + (MIX_T0 + t) // 2)
                    act.activation(halves(tmp[:, t % 2, :]), ps, ACT.Sigmoid).then_inc(sig_done, 1)
                elif t in range(HF, HI):
                    tile_wait(L, t)
                    act.activation(halves(R1[0][:, t - HF, :]), ps, ACT.Sigmoid).then_inc(sig_done, 1)
                    act.activation(halves(kbuf[:, t - HF, :]), ps, ACT.Sigmoid, scale=-1.0).then_inc(free, 1)
                elif t in range(HI, HG) or t in range(GK, GG) or t in range(ML[0], ML[0] + 12):
                    tile_wait(L, t)
                    scale = 1.0
                    if t < HG:
                        dst = R2[0][:, t - HI, :]
                    elif t < GV:
                        dst = R1[1][:, 2 + t - GK, :]
                    elif t < GG:
                        dst = R2[1][:, t - GV, :]
                    else:
                        u = t - ML[0]
                        dst = (R0, R1, R2)[u // 4][2][:, u % 4, :]
                        if u // 4 == 1:
                            scale = float(P) ** -0.5
                    act.activation(halves(dst), ps, ACT.Copy, scale=scale).then_inc(free, 1)
                elif t in range(ML[0] + 12, G1[0]):
                    tile_wait(L, t)
                    act.activation(halves(R3[2][:, t - ML[0] - 12, :]), ps, ACT.Sigmoid).then_inc(free, 1)
                elif t >= G0[0]:
                    m = [t - g[0] for g in (G0, G1, G2) if 0 <= t - g[0] < KT][0]
                    tile_wait(L, t)
                    act.activation(halves(gates[:, m, :]), ps, ACT.Sigmoid).then_inc(free, 1)

            def dma_state(L, i, store):
                if i < 4:
                    d, v = (s_h, st_h), (lambda a: a[L, :, i, :, :].rearrange("b d v -> d b v"))
                elif i < 6:
                    d, v = (s_g, st_g), (lambda a: a[L, :, i - 4, :, :].rearrange("b d v -> d b v"))
                else:
                    d, v = (s_c, st_c), (lambda a: a[L, :, i - 6, :, :].rearrange("b d v -> d b v"))
                if store:
                    act.dma_start(v(d[0]), sst[:, :, :]).then_inc(st_out, 16)
                else:
                    act.dma_start(sst[:, :, :], v(d[1])).then_inc(st_in, 16)

            def step(L, s):
                kind, br, h = s
                no = L * NSTEPS + STEP_NO[s]
                Q, K, V, Tk, O = R0[br], KB[br], R2[br], KTOK[br], OB[br]
                act.wait_ge(pe_step, ONE + no + 1)
                ch.sync()
                if kind == "rows":
                    act.wait_ge(la_1, L + 1)
                    for i in range(2):
                        ch.did(act.activation(halves(setB[:, 4 + i, :]), (SA, SB)[i][:, :, 0:HALF], ACT.Abs,
                                              bias=par[:, P_BG + i:P_BG + i + 1]))
                    ch.did(act.activation(rows[0:4, 2, :], rows[0:4, 1, :], ACT.Abs,
                                          bias=par[0:4, P_BF:P_BF + 1]))
                    ch.sync()
                    ch.link(act.activation(setB[:, 6:8, :], setB[:, 4:6, :], ACT.Exp, scale=-1.0))
                    act.activation(setB[:, 6:8, :], setB[:, 6:8, :], ACT.Ln, bias=1.0).then_inc(la_2, 1)
                    act.wait_ge(la_3, L * 1 + 1)
                    ch.did(act.activation(setB[:, 4:6, :], setB[:, 4:6, :], ACT.Exp, scale=1.0 / 16))
                    ch.link(act.activation(rows[0:4, 2, :], rows[0:4, 2, :], ACT.Exp, scale=-1.0))
                    act.activation(rows[0:4, 2, :], rows[0:4, 2, :], ACT.Ln, bias=1.0).then_inc(row_y, 1)
                    act.wait_ge(row_x, L + 1)
                    ch.did(act.activation(wrow[32:36, :], rows[0:4, 1, :], ACT.Exp))
                    ch.did(act.activation(wrow[64:68, :], rows[0:4, 3, :], ACT.Exp, scale=-1.0))
                    ch.did(act.activation(rows[0:4, 5, :], rows[0:4, 0, :], ACT.Exp))
                elif kind == "v":
                    ch.did(act.activation(V[:, 2 * h:2 * h + 2, 0:SEQ], SA[:, :, :], ACT.Copy))
                    ch.did(act.activation(vts[:, 2 * h:2 * h + 2, :].rearrange("p a b -> p (a b)"),
                                          SB[0:SMP, 0, 0:2 * P], ACT.Copy))
                elif kind == "a":
                    act.wait_ge(d_exp, (L * HEADS + h) + 1)
                    act.activation(att[:, h, 0:SEQ], att[:, h, 0:SEQ], ACT.Exp).then_inc(e_exp, 1)
                    act.activation(att[0:SMP, h, SEQ:TOK], att[0:SMP, h, SEQ:TOK], ACT.Exp).then_inc(e_exp, 1)
                elif kind == "k":
                    nt = 2 if br == 1 else 4
                    if h == 0:
                        for i in range(nt):
                            src = (SA, SB)[i // 2]
                            if br == 2:
                                for c in range(NCH):
                                    cs = slice(c * CH, (c + 1) * CH)
                                    ch.did(act.activation(Tk[:, i, cs], src[:, i % 2, cs], ACT.Copy,
                                                          scale=colW[:, c * 4 + i:c * 4 + i + 1]))
                            elif i % 2 == 0:
                                ch.did(act.activation(Tk[:, i:i + 2, 0:SEQ], src[:, :, :], ACT.Copy))
                    elif br == 2:
                        for i in range(nt):
                            ch.did(act.activation(kts[:, i, :], SA[0:SMP, 0, i * P:(i + 1) * P], ACT.Copy,
                                                  scale=colS[:, 4 + i:5 + i]))
                    else:
                        ch.did(act.activation(kts[:, 0:nt, :].rearrange("p a b -> p (a b)"),
                                              SA[0:SMP, 0, 0:nt * P], ACT.Copy))
                elif kind == "ns":
                    ch.link(act.activation(nOt[:, :], SA[0:SMP + HEADS, 0, 0:P], ACT.Copy))
                    act.dma_start(s_n[L, :, :], nOt[0:SMP, :]).then_inc(out_sem, 16)
                    act.dma_start(p_n[L, :, :], nOt[SMP:SMP + HEADS, :]).then_inc(out_sem, 16)
                elif kind == "m":
                    ch.did(act.activation(tmp[:, 3, 0:SEQ], SA[:, 0, :], ACT.Copy))
                    ch.did(act.activation(tmp[:, 3, SEQ:TOK], SA[:, 1, 0:SMP], ACT.Copy))
                elif kind == "o":
                    if h == 0:
                        act.wait_ge(dve_step, ONE + L * NSTEPS + (STEP_NO[("u", br, 0)] + 1))
                        for i in range(2 if br == 1 else 4):
                            dst = (p_h, p_g, p_c)[br]
                            act.dma_start(dst[L, i, :, :], K[:, i, 3 * CH:4 * CH]).then_inc(out_sem, 16)
                    if br == 2:
                        act.activation(tmp[:, 5, 0:SEQ], SB[:, 0, :], ACT.Abs).then_inc(d_abs, 1)
                        act.activation(tmp[:, 5, SEQ:TOK], SB[:, 1, 0:SMP], ACT.Abs).then_inc(d_abs, 1)
                    if br < 2:
                        ch.did(act.activation(O[:, h, 0:SEQ], SA[:, 0, :], ACT.Copy))
                        ch.did(act.activation(O[:, h, SEQ:TOK], SA[:, 1, 0:SMP], ACT.Copy))
                        ch.did(act.activation(tmp[:, 2, 0:SEQ], SA[:, 0, :], ACT.Square))
                        ch.did(act.activation(tmp[:, 2, SEQ:TOK], SA[:, 1, 0:SMP], ACT.Square))
                elif kind == "n":
                    if br != 1 or h % 2 == 1:
                        i = st_no(br, h)
                        act.wait_ge(dve_step, ONE + L * NSTEPS + (STEP_NO[("z", br, h)] + 1))
                        dma_state(L, i, True)
                    idx = L * 12 + (br * 4 + h)
                    ch.link(act.activation(halves(tmp[:, 5, :]), SB[:, :, 0:HALF], ACT.Ln, bias=epsc[:, :],
                                           scale=1.0 / P))
                    act.activation(tmp[:, 5, :], tmp[:, 5, :], ACT.Exp, scale=-0.5).then_inc(h_rs, 1)
                    act.wait_ge(h_of, idx + 1)
                    act.activation(OH[br][:, h, :], O[:, h, :], ACT.Copy).then_inc(h_hi, 1)
                    if (br != 1 or h % 2 == 1) and i < 9:
                        act.wait_ge(st_out, L * 160 + 16 * (i + 1))
                        dma_state(L, i + 1, False)
                ch.sync()
                act.sem_inc(act_step, 1)

            act.dma_start(const[:, :], const_d).then_inc(consts_in, 16)
            act.dma_start(parL[:, :, :], par_d).then_inc(consts_in, 16)
            act.dma_start(kbuf[:, 0:2, 0:448], lvm_d).then_inc(consts_in, 16)
            act.dma_start(lbt[:, 0:8], lb_d).then_inc(consts_in, 16)
            act.dma_start(fg[:, :], fg_d).then_inc(consts_in, 16)
            act.dma_start(X[:, :, :], xT).then_inc(x_in, 16)
            act.wait_ge(const_ready, 1)
            act.activation(lbt[:, 8:16], lbt[:, 8:16], ACT.Exp).then_inc(const_ready, 1)
            with act.Fori(0, DEPTH) as L:
                outer = ch.loop(L, 1024)
                ffn(L, 0, L * 3, 0)
                act_norm(L * 3 + 1)
                act.dma_start(x_keep, X[:, :, :]).then_inc(x_read, 16)
                act.dma_start(nst[0:SMP, :], st_n[L, :, :]).then_inc(m_in, 16)
                act.dma_start(m0[:, :], st_m[L, :, :]).then_inc(m_in, 16)
                dma_state(L, 0, False)
                for s in ORDER:
                    if s[0] == "tile":
                        tile(L, s[1])
                    elif s[0] == "out":
                        act.dma_start(s_m[L, :, :], mO[:, :]).then_inc(out_sem, 16)
                        for m in range(KT):
                            act.wait_ge(mg_f, (L * KT + m) + 1)
                            act.activation(Hh[:, m, :], X[:, m, :], ACT.Copy).then_inc(mg_hi, 1)
                        act.wait_ge(mg_lo, (L + 1) * KT)
                        act.wait_ge(x_read, L * 32 + 16)
                        act.dma_start(X[:, :, :], x_keep).then_inc(x_read, 16)
                    elif s[0] != "branch":
                        step(L, s)
                act.wait_ge(out_sem, (L + 1) * (16 * 13))
                act.wait_ge(st_out, (L + 1) * 160)
                ffn(L, FFN2_T0, L * 3 + 2, 1)
                ch.end(outer, 1024, DEPTH)
            act_norm(3 * DEPTH, final=True)
            for k in range(KT):
                act.wait_ge(y_ready, k + 1)
                act.dma_start(yT[:, k, :], X[:, k, :]).then_inc(y_out, 16)
            act.wait_ge(y_out, 16 * KT)

        @block.vector
        def _(dve):
            ch = Chain(dve, dlink)
            dve.sem_inc(dlink, ONE)
            dve.sem_inc(dve_step, ONE)
            dve.sem_inc(slot_free[1], ONE)
            TT, TS, STT = dve.tensor_tensor, dve.tensor_scalar, dve.scalar_tensor_tensor

            def square_sum(m):
                ch.sync()
                ch.link(TT(tmp[:, 4:5, :], X[:, m, :], X[:, m, :], ALU.mult))
                ch.did(TT(tmp[:, 3:4, :], tmp[:, 3:4, :], tmp[:, 4:5, :], ALU.add))

            def ssq_start():
                ch.did(dve.memset(tmp[:, 3, :], 0.0))

            def ssq_end():
                ch.sync()
                dve.sem_inc(ssq_ready, 1)

            def norm(n, g0):
                dve.wait_ge(rs_ready, n + 1)
                for k in range(KT + 1):
                    if k < KT:
                        if k > 1:
                            dve.wait_ge(norm_lo, n * KT + (k - 1))
                        STT(tmp[:, k % 2, :], X[:, k, :], par[:, g0 + k:g0 + k + 1], tmp[:, 2, :],
                            ALU.mult, ALU.mult).then_inc(norm_h, 1)
                    if k:
                        dve.wait_ge(norm_hi, n * KT + k)
                        TT(Hl[:, k - 1, :], tmp[:, (k - 1) % 2, :], f32(Hh[:, k - 1, :]),
                           ALU.subtract).then_inc(norm_lo, 1)

            def ffn(L, t0, norm_no, which, g0):
                norm(norm_no, g0)
                for b, nf in enumerate((FF_BLOCK, FF_BLOCK, FF_LAST)):
                    off = b * 24
                    with dve.Fori(0, nf // 2) as i:
                        for j in range(2):
                            use = L * (TILES // 2) + ((t0 + off) // 2 + j + 1) + i * 2
                            f = L * (2 * FF_TILES) + (which * FF_TILES + b * FF_BLOCK + j) + i * 2
                            dve.wait_ge(slot_free[0], ONE + use)
                            dve.wait_ge(tile_done, ONE + L * TILES + (t0 + off + 2 * j + 2) + i * 4)
                            TT(halves(tmp[:, j, :]), dps[1][:, :, 0:HALF], halves(tmp[:, 4 + j, :]),
                               ALU.mult).then_inc(slot_free[1], 1)
                            dve.wait_ge(ffn_hi, f + 1)
                            TT(Al[:, bass.ds(i * 2 + j, 1), :], tmp[:, j:j + 1, :],
                               f32(Ah[:, bass.ds(i * 2 + j, 1), :]), ALU.subtract).then_inc(ffn_lo, 1)
                    if b == 2:
                        ssq_start()
                    with dve.Fori(0, 2) as i:
                        outer = ch.loop(i, 16)
                        for j in range(4):
                            dve.wait_ge(tile_done, ONE + L * TILES + (t0 + off + 2 * nf + j + 1) + i * 4)
                            xs = X[:, bass.ds(i * 4 + j, 1), :].rearrange("p a (b c) -> p (a b) c", b=2)
                            STT(xs, dps[j % 2][:, :, 0:HALF], 0.5, xs, ALU.mult,
                                ALU.add).then_inc(slot_free[j % 2], 1)
                            if b == 2:
                                dve.wait_ge(slot_free[j % 2],
                                            ONE + L * (TILES // 2) + ((t0 + off + 2 * nf) // 2 + j // 2 + 1) + i * 2)
                                square_sum(bass.ds(i * 4 + j, 1))
                        ch.end(outer, 16, 2)
                ssq_end()

            def tile(L, t):
                g = MIX_T0 + t
                slot = g % 2
                ps = dps[slot][:, :, 0:HALF]
                free = slot_free[slot]
                silu_no = ([*range(HQ, HF), *range(HF, HI), *range(HG, SMALL), *range(GG, G0[0])])
                if t in silu_no:
                    dve.wait_ge(sig_done, L * 16 + (silu_no.index(t) + 1))
                    if t in range(HF, HI):
                        i = t - HF
                        dve.wait_ge(free, ONE + L * (TILES // 2) + (g // 2 + 1))
                        ch.did(TS(kbuf[:, i, :], kbuf[:, i, :], lbc[:, 4 + i:5 + i], None, ALU.mult))
                        ch.did(TS(R1[0][:, i, :], R1[0][:, i, :], lbc[:, 4 + i:5 + i], lbc[:, i:i + 1],
                                  ALU.mult, ALU.add))
                        return
                    dst = (R0[0][:, t, :] if t < HF else R3[0][:, t - HG, :] if t < SMALL
                           else R3[1][:, t - GG, :])
                    TT(halves(dst), ps, halves(tmp[:, t % 2, :]), ALU.mult).then_inc(free, 1)
                elif t == SMALL:
                    dve.wait_ge(tile_done, ONE + L * TILES + (g + 1))
                    ch.did(dve.tensor_copy(halves(glr[:, :]), dps[slot][0:16, :, 0:HALF]))
                    ch.did(dve.tensor_copy(halves(rows[0:4, 0, :]), dps[slot][32:36, :, 0:HALF]))
                    ch.did(dve.tensor_copy(halves(rows[0:4, 1, :]), dps[slot][64:68, :, 0:HALF]))
                    ch.sync()
                    dve.sem_inc(free, 1)
                    dve.sem_inc(lr_used, 2)
                elif t in range(GQ, GK):
                    i = t - GQ
                    dve.wait_ge(tile_done, ONE + L * TILES + (g + 1))
                    for e in range(2):
                        ins = TS(halves(R0[1][64 * e:64 * e + 64, 2 * i + e, :]),
                                 dps[slot][64 * e:64 * e + 64, :, 0:HALF], 0.125, None, ALU.mult)
                        ch.did(ins)
                    ch.sync()
                    dve.sem_inc(free, 1)

            def tree(ap, op, width, levels, first=1):
                for l in range(first, levels + 1):
                    bs, hf = 1 << l, 1 << (l - 1)
                    v = ap[:, 0:width].rearrange("p (n b) -> p n b", b=bs)
                    ch.link(TT(v[:, :, hf:bs], v[:, :, hf:bs],
                               v[:, :, hf - 1:hf].to_broadcast([HEADS, width // bs, hf]), op))

            def rows_step(L):
                z = setB
                for i in range(2):
                    bias = par[:, P_BG + i:P_BG + i + 1]
                    bank = (SA, SB)[i][:, :, 0:HALF]
                    ch.did(TS(halves(z[:, i, :]), bank, bias, 0.0, ALU.add, ALU.min))
                ch.sync()
                dve.sem_inc(la_1, 1)
                r = rows
                bi, bf = par[0:4, P_BI:P_BI + 1], par[0:4, P_BF:P_BF + 1]
                ch.did(TS(r[0:4, 3, :], r[0:4, 1, :], bf, 0.0, ALU.add, ALU.min))
                dve.wait_ge(la_2, L * 1 + 1)
                ch.did(TT(z[:, 4:6, :], z[:, 0:2, :], z[:, 6:8, :], ALU.subtract))
                ch.sync()
                dve.sem_inc(la_3, 1)
                for e in range(2):
                    q = setB[64 * (1 - e):64 * (1 - e) + 64, e:4:2, :]
                    ch.did(dve.memset(q, 0.0))
                dve.wait_ge(row_y, L * 1 + 1)
                ch.link(TT(r[0:4, 1, :], r[0:4, 3, :], r[0:4, 2, :], ALU.subtract))
                tree(r[0:4, 1, :], ALU.add, TOK, S_LEVELS)
                tree(r[0:4, 1, :], ALU.add, SEQ, LEVELS, S_LEVELS + 1)
                ch.link(STT(r[0:4, 4, :], r[0:4, 0, :], bi, r[0:4, 1, :], ALU.add, ALU.subtract))
                ch.link(dve.tensor_copy(r[0:4, 2, :], r[0:4, 4, :]))
                tree(r[0:4, 2, :], ALU.max, TOK, S_LEVELS)
                tree(r[0:4, 2, :], ALU.max, SEQ, LEVELS, S_LEVELS + 1)
                ch.link(dve.memset(mch[:, 0:1], 0.0))
                for c in range(NCH):
                    cs, e = slice(c * CH, (c + 1) * CH), (c + 1) * CH - 1
                    ch.link(TS(r[0:4, 2, cs], r[0:4, 2, cs], mch[:, c:c + 1], None, ALU.max))
                    ch.did(TT(mch[:, c + 1:c + 2], r[0:4, 2, e:e + 1], r[0:4, 1, e:e + 1], ALU.add))
                    ch.sync()
                dve.wait_ge(m_in, L * 32 + 32)
                sv = [r[0:4, i, SEQ:TOK].rearrange("p (b t) -> p b t", t=DEC_T) for i in range(6)]
                m0b = m0[:, :].unsqueeze(2).to_broadcast([HEADS, DEC_B, DEC_T])
                ch.link(TT(sv[2], sv[2], m0b, ALU.max))
                ch.did(TT(mO[:, 1:].unsqueeze(2), sv[2][:, :, 3:4], sv[1][:, :, 3:4], ALU.add))
                ch.did(dve.tensor_copy(mO[:, 0:1], mch[:, NCH:NCH + 1]))
                ch.did(TT(r[0:4, 3, :], r[0:4, 1, :], r[0:4, 2, :], ALU.add))
                ch.sync()
                for c in range(NCH):
                    cs, e = slice(c * CH, (c + 1) * CH), (c + 1) * CH - 1
                    ch.did(TS(r[0:4, 1, cs], r[0:4, 2, cs], -1.0, mch[:, c:c + 1], ALU.mult, ALU.add))
                    ch.did(TS(r[0:4, 0, cs], r[0:4, 4, cs], r[0:4, 2, e:e + 1], None, ALU.subtract))
                ch.did(TT(sv[1], m0b, sv[2], ALU.subtract))
                ch.did(TT(sv[0], sv[4], sv[2][:, :, 3:4].to_broadcast([HEADS, DEC_B, DEC_T]), ALU.subtract))
                ch.did(TS(wrow[0:4, :], r[0:4, 2, :], -1.0, None, ALU.mult))
                ch.sync()
                dve.sem_inc(row_x, 1)

            def qkt_update(br, l):
                w = TOK if l <= S_LEVELS else SEQ
                bs, hf = 1 << l, 1 << (l - 1)

                def bl(ap):
                    return ap[:, :, 0:w].rearrange("p h (n b) -> p h n b", b=bs)

                T = R1[br] if br == 0 else R1[1][:, 0:2, :]
                for e in range(1 if br == 0 else 2):
                    n, ps, hs = (P, slice(0, P), slice(0, 4)) if br == 0 else (64, slice(64 * e, 64 * e + 64),
                                                                              slice(e, 4, 2))
                    q, t = bl(R0[br][ps, hs, :]), bl(T[ps])
                    ch.did(TT(q[:, :, :, hf:bs], q[:, :, :, hf:bs],
                              t[:, :, :, 0:1].to_broadcast([n, t.shape[1], w // bs, hf]), ALU.mult))
                k, t = bl(KB[br]), bl(T)
                ch.did(TT(k[:, :, :, 0:hf], k[:, :, :, 0:hf],
                          t[:, :, :, hf:hf + 1].to_broadcast([P, t.shape[1], w // bs, hf]), ALU.mult))
                ch.sync()
                t = bl(T)
                ch.did(TT(t[:, :, :, 0], t[:, :, :, 0], t[:, :, :, hf], ALU.mult))
                ch.sync()

            def step(L, s):
                kind, br, h = s
                no = L * NSTEPS + STEP_NO[s]
                Q, K, V, Tk, O = R0[br], KB[br], R2[br], KTOK[br], OB[br]
                nt = 2 if br == 1 else 4
                dve.wait_ge(pe_step, ONE + no + 1)
                ch.sync()
                if kind == "rows":
                    rows_step(L)
                elif kind == "cols":
                    ch.did(dve.tensor_copy(colG[:, :], SA[:, 0, 0:16]))
                    ch.did(dve.tensor_copy(colW[:, :], SA[:, 0, 32:48]))
                    ch.did(dve.tensor_copy(colS[:, 0:4], SA[0:SMP, 1, 0:4]))
                    ch.did(dve.tensor_copy(colS[:, 4:8], SA[0:SMP, 1, 32:36]))
                    ch.did(dve.tensor_copy(nS[:, :], SB[:, 0, 0:SMP]))
                elif kind == "d":
                    a = att[:, 2 * h:2 * h + 2, 0:SEQ].rearrange("p h (c t) -> p h c t", t=CH)
                    ch.did(TT(a, SA[:, :, :].rearrange("p h (c t) -> p h c t", t=CH),
                              diag.unsqueeze(1).unsqueeze(1).to_broadcast([P, 2, NCH, CH]), ALU.mult))
                    if h == 0:
                        ch.did(TT(att[0:SMP, :, SEQ:TOK],
                                  SB[0:SMP, 0, 0:4 * SMP].rearrange("p (h t) -> p h t", t=SMP),
                                  diag[0:SMP, 0:SMP].unsqueeze(1).to_broadcast([SMP, 4, SMP]), ALU.mult))
                    else:
                        if br == 0:
                            ch.did(TT(Q, Q, R1[0], ALU.mult))
                        else:
                            for e in range(2):
                                q = Q[64 * e:64 * e + 64, e:4:2, :]
                                ch.did(TT(q, q, R1[1][64 * e:64 * e + 64, 0:2, :], ALU.mult))
                elif kind == "lv":
                    dve.sem_inc(dve_began, 1)
                    bs, hf = 1 << h, 1 << (h - 1)
                    mk = mask(h).rearrange("p (n b) -> p n b", b=bs)[:, :, hf:bs]
                    for s0 in range(0, CH if hf >= 32 else 1, bs):
                        if hf >= 32:
                            n0 = s0 // bs * hf
                            a = att[s0:s0 + hf, :, 0:SEQ].rearrange("p h (c t) -> p h c t", t=CH)
                            src = SA[s0:s0 + hf, :, :].rearrange("p a (b c t) -> p (a b) c t", b=2, c=NCH)
                            ch.did(dve.tensor_copy(a[:, :, :, s0 + hf:s0 + bs], src[:, :, :, n0:n0 + hf]))
                    for i in range(HEADS if hf < 32 else 0):
                        a = att[:, i, 0:SEQ].rearrange("p (c n b) -> p c n b", c=NCH, b=bs)
                        src = SA[:, i // 2, (i % 2) * 256:(i % 2) * 256 + 256]
                        ch.did(dve.copy_predicated(a[:, :, :, hf:bs],
                                                   mk.unsqueeze(1).to_broadcast([P, NCH, CH // bs, hf]),
                                                   src.rearrange("p (c n b) -> p c n b", c=NCH, b=hf)))
                    if h <= S_LEVELS:
                        ch.did(dve.copy_predicated(
                            att[0:SMP, :, SEQ:TOK],
                            mask(h)[0:SMP, 0:SMP].unsqueeze(1).to_broadcast([SMP, 4, SMP]),
                            SB[0:SMP, 0, 0:4 * SMP].rearrange("p (h t) -> p h t", t=SMP)))
                    qkt_update(br, h)
                    if h == LEVELS:
                        T = R1[br][:, 0:nt, :]
                        ch.did(dve.tensor_copy(dec[:, 0:nt, :], T[:, :, 0:SEQ:CH]))
                        ch.did(dve.tensor_copy(decs[:, 0:nt, :], T[:, :, SEQ:TOK:DEC_T]))
                elif kind == "a":
                    for c in range(NCH):
                        cs = slice(c * CH, (c + 1) * CH)
                        ch.did(STT(att[:, h, cs], SA[:, 0, cs], colG[:, c * 4 + h:c * 4 + h + 1],
                                   const[:, C_NEG:C_NEG + 128], ALU.add, ALU.min))
                    ch.did(STT(att[0:SMP, h, SEQ:TOK], SB[0:SMP, 0, 0:32], colS[:, h:h + 1],
                               const[0:SMP, C_NEGS:C_NEGS + 32], ALU.add, ALU.min))
                    ch.sync()
                    dve.sem_inc(d_exp, 1)
                    ch.did(TT(Q[:, h, 0:SEQ], Q[:, h, 0:SEQ], SB[:, 1, :], ALU.mult))
                    ch.did(TT(Q[:, h, SEQ:TOK], Q[:, h, SEQ:TOK], SB[:, 0, 64:96], ALU.mult))
                    ch.did(dve.tensor_copy(dec[:, h, :], SB[:, 1, CH - 1:SEQ:CH]))
                    ch.did(dve.tensor_copy(decs[:, h, :], SB[:, 0, 64 + DEC_T - 1:96:DEC_T]))
                    dve.wait_ge(e_exp, (L * HEADS + h) * 2 + 2)
                    ch.did(TT(att[:, h, 0:SEQ], att[:, h, 0:SEQ], SA[:, 1, :], ALU.mult))
                    ch.did(TT(att[0:SMP, h, SEQ:TOK], att[0:SMP, h, SEQ:TOK], SB[0:SMP, 0, 32:64], ALU.mult))
                elif kind == "u":
                    for i in range(nt):
                        ch.did(dve.tensor_copy(K[:, i, 0:CH], (SA, SB)[i // 2][:, i % 2, 0:CH]))
                    for c in range(1, NCH):
                        ch.sync()
                        for i in range(nt):
                            cs, ps = slice(c * CH, (c + 1) * CH), slice((c - 1) * CH, c * CH)
                            ch.did(STT(K[:, i, cs], K[:, i, ps], dec[:, i, c:c + 1],
                                       (SA, SB)[i // 2][:, i % 2, cs], ALU.mult, ALU.add))
                elif kind == "un":
                    U = SA[:, 0, 0:16].rearrange("p (h c) -> p h c", c=4)
                    ch.link(dve.tensor_copy(nP[:, :, 0:1], U[:, :, 0:1]))
                    for c in range(1, NCH):
                        ch.link(TT(nP[:, :, c:c + 1], nP[:, :, c - 1:c], dec[:, :, c:c + 1], ALU.mult))
                        ch.link(TT(nP[:, :, c:c + 1], nP[:, :, c:c + 1], U[:, :, c:c + 1], ALU.add))
                    v = nO[:, 0:SMP].rearrange("p (b h) -> p b h", h=4)
                    ch.link(TT(v, nS[:, :].rearrange("p (b h) -> p b h", h=4),
                               decs[:, :, :].rearrange("p h b -> p b h"), ALU.mult))
                    ch.link(TT(v, v, SA[:, 0, 64:96].rearrange("p (h b) -> p b h", b=8), ALU.add))
                    ch.did(dve.tensor_copy(nO[:, SMP:SMP + HEADS], nP[:, :, NCH - 1]))
                elif kind == "m":
                    for c in range(1, NCH):
                        cs = slice(c * CH, (c + 1) * CH)
                        ch.did(TS(tmp[:, 5, cs], Q[:, h, cs], nP[:, h, c - 1:c], None, ALU.mult))
                    ch.did(TT(tmp[:, 5, SEQ:TOK].rearrange("p (b t) -> p b t", t=DEC_T),
                              Q[:, h, SEQ:TOK].rearrange("p (b t) -> p b t", t=DEC_T),
                              nS[:, h:SMP:4].unsqueeze(2).to_broadcast([P, DEC_B, DEC_T]), ALU.mult))
                elif kind == "o":
                    if br == 2:
                        nb = tmp[:, 3, :]
                        dve.wait_ge(d_abs, (L * HEADS + h) * 2 + 2)
                        ch.link(TT(nb, nb, tmp[:, 5, :], ALU.max))
                        ch.link(dve.reciprocal(nb, nb))
                        ch.did(TT(O[:, h, 0:SEQ], SA[:, 0, :], nb[:, 0:SEQ], ALU.mult))
                        ch.did(TT(O[:, h, SEQ:TOK], SA[:, 1, 0:SMP], nb[:, SEQ:TOK], ALU.mult))
                        ch.sync()
                        ch.did(TT(tmp[:, 2, :], O[:, h, :], O[:, h, :], ALU.mult))
                    ch.did(TT(vblk[:, :].rearrange("p (b v) -> p b v", v=P),
                              vts[:, h, :].unsqueeze(1).to_broadcast([SMP, DEC_B, P]),
                              const[0:SMP, C_BM:C_BM + 8].unsqueeze(2).to_broadcast([SMP, DEC_B, P]), ALU.mult))
                elif kind == "z":
                    sl = slice(64 * (h % 2), 64 * (h % 2) + 64) if br == 1 else slice(0, P)
                    n = 64 if br == 1 else P
                    ch.link(TT(sst[sl], sst[sl],
                               decs[sl, kt(br, h), :].unsqueeze(2).to_broadcast([n, DEC_B, P]), ALU.mult))
                    ch.did(TT(sst[sl].rearrange("p (a b) v -> p a (b v)", a=2),
                              sst[sl].rearrange("p (a b) v -> p a (b v)", a=2), SB[sl, :, :], ALU.add))
                elif kind == "n":
                    idx = L * 12 + (br * 4 + h)
                    dve.wait_ge(h_rs, idx + 1)
                    ch.link(STT(O[:, h, :], O[:, h, :], par[:, P_HN + br:P_HN + br + 1], tmp[:, 5, :],
                                ALU.mult, ALU.mult))
                    TT(O[:, h, :], O[:, h, :], R3[br][:, h, :], ALU.mult).then_inc(h_of, 1)
                    dve.wait_ge(h_hi, idx + 1)
                    TT(OL[br][:, h, :], O[:, h, :], f32(OH[br][:, h, :]), ALU.subtract).then_inc(h_lo, 1)
                    dve.wait_ge(h_lo, idx + 1)
                ch.sync()
                dve.sem_inc(dve_step, 1)

            def branch(L, br, m):
                if br == 0 and m == 0:
                    dve.wait_ge(x_read, L * 32 + 16)
                g = MIX_T0 + (B0, B1, B2)[br][0] + m
                slot = g % 2
                dve.wait_ge(tile_done, ONE + L * TILES + (g + 1))
                gt = MIX_T0 + (G0, G1, G2)[br][0] + m
                dve.wait_ge(slot_free[gt % 2], ONE + L * (TILES // 2) + (gt // 2 + 1))
                dst = X if br == 0 else gates
                TT(halves(dst[:, m, :]), dps[slot][:, :, 0:HALF], halves(gates[:, m, :]),
                   ALU.mult).then_inc(slot_free[slot], 1)
                if br:
                    dve.wait_ge(slot_free[slot], ONE + L * (TILES // 2) + (g // 2 + 1))
                    ins = TT(X[:, m, :], X[:, m, :], gates[:, m, :], ALU.add)
                    if br == 1:
                        ch.did(ins)
                    else:
                        ins.then_inc(mg_f, 1)
                        if m:
                            merged_lo(L, m - 1)
                        if m == KT - 1:
                            merged_lo(L, m)

            def merged_lo(L, m):
                dve.wait_ge(mg_hi, (L * KT + m) + 1)
                TT(Hl[:, m, :], X[:, m, :], f32(Hh[:, m, :]), ALU.subtract).then_inc(mg_lo, 1)

            ch.did(dve.memset(ones[:, :], 1.0))
            ch.did(dve.memset(epsc[:, :], EPS))
            ch.did(dve.memset(wrow[:, :], 0.0))
            dve.wait_ge(consts_in, 80)
            a, b = lbt[:, 0:4], lbt[:, 4:8]
            ch.did(dve.tensor_copy(lvm[:, :].rearrange("p (a b) -> p a b", a=2), kbuf[:, 0:2, 0:448]))
            ch.link(TT(lbt[:, 16:20], a, b, ALU.max))
            ch.did(TT(lbt[:, 8:12], a, lbt[:, 16:20], ALU.subtract))
            ch.did(TT(lbt[:, 12:16], b, lbt[:, 16:20], ALU.subtract))
            ch.sync()
            dve.sem_inc(const_ready, 1)
            dve.wait_ge(const_ready, 2)
            ch.link(TT(lbt[:, 16:20], lbt[:, 8:12], lbt[:, 12:16], ALU.add))
            ch.link(dve.reciprocal(lbt[:, 16:20], lbt[:, 16:20]))
            ch.did(TT(lbt[:, 8:12], lbt[:, 8:12], lbt[:, 16:20], ALU.mult))
            ch.did(TT(lbt[:, 12:16], lbt[:, 12:16], lbt[:, 16:20], ALU.mult))
            ch.sync()
            ch.link(TT(lbs[:, 1, :], lbt[:, 8:12], lbt[:, 12:16], ALU.add))
            ch.did(TT(lbs[:, 0, :], lbt[:, 8:12], lbt[:, 8:12], ALU.subtract))
            ch.did(TT(lbs[:, 1, :], lbs[:, 1, :], lbt[:, 8:12], ALU.subtract))
            dve.wait_ge(x_in, 16)
            ssq_start()
            for m in range(KT):
                square_sum(slice(m, m + 1))
            ssq_end()
            with dve.Fori(0, DEPTH) as L:
                outer = ch.loop(L, 1024)
                ch.did(dve.tensor_copy(par[:, 0:31].unsqueeze(1), parL[:, bass.ds(L, 1), :]))
                ch.did(dve.tensor_copy(par[0:16, P_LR:NPAR], const[96:112, bass.ds(L * 256 + C_SEL, 256)]))
                ch.did(dve.tensor_copy(lbc[:, 0:4].unsqueeze(1), lbs[:, bass.ds(L, 1), :]))
                ch.sync()
                ch.did(TS(lbc[:, 4:8], lbc[:, 0:4], -1.0, 1.0, ALU.mult, ALU.add))
                ch.sync()
                ffn(L, 0, L * 3, 0, PG["ffn1"])
                norm(L * 3 + 1, PG["mix"])
                for s in ORDER:
                    if s[0] == "tile":
                        tile(L, s[1])
                    elif s[0] == "branch":
                        branch(L, s[1], s[2])
                    elif s[0] != "out":
                        step(L, s)
                ssq_start()
                dve.wait_ge(x_read, L * 32 + 32)
                for m in range(KT):
                    g = MIX_T0 + WO[0] + m
                    dve.wait_ge(tile_done, ONE + L * TILES + (g + 1))
                    TT(halves(X[:, m, :]), dps[g % 2][:, :, 0:HALF], halves(X[:, m, :]),
                       ALU.add).then_inc(slot_free[g % 2], 1)
                    dve.wait_ge(slot_free[g % 2], ONE + L * (TILES // 2) + (g // 2 + 1))
                    square_sum(slice(m, m + 1))
                ssq_end()
                dve.wait_ge(tile_done, ONE + L * TILES + FFN2_T0)
                dve.sem_inc(slot_free[1], 1)
                ffn(L, FFN2_T0, L * 3 + 2, 1, PG["ffn2"])
                ch.end(outer, 1024, DEPTH)
            dve.wait_ge(rs_ready, 3 * DEPTH + 1)
            for k in range(KT):
                STT(X[:, k, :], X[:, k, :], fg[:, k:k + 1], tmp[:, 2, :], ALU.mult, ALU.mult).then_inc(y_ready, 1)


def _tiles(w):
    return w.reshape(w.shape[0] // P, P, w.shape[1] // P, P).transpose(0, 2, 1, 3)


def weight_stream(a):
    out = np.zeros((DEPTH, PIECES, P, 8, P), np.float32)
    for l in range(DEPTH):
        n = 0

        def put(tiles, at=0):
            nonlocal n
            out[l, n, :, at:at + tiles.shape[0], :] = tiles.transpose(1, 0, 2)

        def ffn(up, down):
            nonlocal n
            up, down = _tiles(up), _tiles(down)
            for f0, nf in ((0, FF_BLOCK), (FF_BLOCK, FF_BLOCK), (2 * FF_BLOCK, FF_LAST)):
                for f in range(f0, f0 + nf):
                    put(up[:, f]); n += 1
                    put(up[:, FF_TILES + f]); n += 1
                for m in range(KT):
                    put(down[f0:f0 + nf, m]); n += 1

        ffn(a["ffn1_w_up"][l], a["ffn1_w_down"][l])
        w = a["w_in"][l]
        sizes = [512] * 4 + [256, 256, 512, 512, 16] + [512] * 4 + [4, 4, 3072]
        at = np.cumsum([0] + sizes)
        part = [w[:, at[i]:at[i + 1]] for i in range(len(sizes))]
        small = np.zeros((D_MODEL, P), np.float32)
        small[:, 0:16], small[:, 32:36], small[:, 64:68] = part[8], part[13], part[14]

        def proj(x):
            nonlocal n
            for i in range(x.shape[1] // P):
                put(_tiles(x)[:, i]); n += 1

        def gate(b):
            proj(part[15][:, b * D_MODEL:(b + 1) * D_MODEL])

        def branch(b):
            nonlocal n
            t = _tiles(a["w_branch"][l, b])
            for m in range(0, KT, 2):
                put(t[:, m]); put(t[:, m + 1], 4); n += 1

        for i in (0, 1, 2, 3):
            proj(part[i])
        proj(small)
        for i in (4, 5, 6, 7):
            proj(part[i])
        gate(0); branch(0)
        for i in (9, 10, 11, 12):
            proj(part[i])
        gate(1); branch(1); gate(2); branch(2)
        proj(a["w_out"][l])
        n += 3
        ffn(a["ffn2_w_up"][l], a["ffn2_w_down"][l])
        assert n == PIECES
    return out.reshape(DEPTH * PIECES, P, 1024)


def constants():
    c = np.zeros((P, NCONST), np.float32)
    m = np.zeros((P, LEVELS * P), np.float32)
    i = np.arange(P)
    s, t = i[:, None], i[None, :]
    c[:, C_ID:C_ID + P] = s == t
    c[:, C_DIAG:C_DIAG + P] = s == t
    for l in range(1, LEVELS + 1):
        b, hf = 1 << l, 1 << (l - 1)
        m[:, (l - 1) * P:l * P] = (s // b == t // b) & (s % b < hf) & (t % b >= hf)
    c[:, C_NEG:C_NEG + P] = np.where(s <= t, 0.0, -1e30)
    c[0:SMP, C_NEGS:C_NEGS + SMP] = np.where((s <= t) & (s // DEC_T == t // DEC_T), 0.0, -1e30)[0:SMP, 0:SMP]
    for q in range(3):
        for h in range(HEADS):
            c[32 * q + h, C_SEL + h * P:C_SEL + (h + 1) * P] = 1.0
    c[0:SMP, C_BM:C_BM + DEC_B] = np.arange(SMP)[:, None] // DEC_T == np.arange(DEC_B)[None, :]
    return c, m


def kernel(**inputs):
    import concourse.bacc as bacc
    from concourse.bass_utils import run_bass_kernel_spmd

    a = {k: np.asarray(v) for k, v in inputs.items()}

    def cols(v, n):
        return v.reshape(DEPTH, n, P).transpose(2, 0, 1)

    par = np.zeros((P, DEPTH, P_LR), np.float32)
    par[:, :, 0:8] = cols(a["ffn1_norm"], 8)
    par[:, :, 8:16] = cols(a["mix_norm"], 8)
    par[:, :, 16:24] = cols(a["ffn2_norm"], 8)
    for i, name in enumerate(("hgrn_out_norm", "gla_out_norm", "mlstm_out_norm")):
        par[:, :, P_HN + i] = a[name].T
    par[:, :, P_BG:P_BG + 2] = cols(a["gla_b_gate"], 2)
    par[0:4, :, P_BI], par[0:4, :, P_BF] = a["mlstm_b_i"].T, a["mlstm_b_f"].T
    const, lvm = constants()
    const[96:112, C_SEL:C_SEL + 512] = a["gla_w_gate_lr"].transpose(1, 0, 2).reshape(16, 512)
    xs = np.concatenate([a["x_prompt"].reshape(SEQ, D_MODEL), a["x_sample"].reshape(SMP, D_MODEL)])
    arrays = {
        "wst": weight_stream(a),
        "xT": np.ascontiguousarray(xs.T.reshape(KT, P, TOK).transpose(1, 0, 2)),
        "par": par,
        "lb": np.ascontiguousarray(cols(a["hgrn_lb_raw"], 4).reshape(P, 8)),
        "const": const,
        "lvm": lvm.reshape(P, 2, 448),
        "fg": np.ascontiguousarray(a["final_norm"].reshape(KT, P).T),
        "st_h": a["state_hgrn"],
        "st_g": a["state_gla"].reshape(DEPTH, DEC_B, 2, P, P),
        "st_c": a["state_mlstm_C"],
        "st_n": a["state_mlstm_n"].reshape(DEPTH, SMP, P),
        "st_m": np.ascontiguousarray(a["state_mlstm_m"].transpose(0, 2, 1)),
    }
    nc = bacc.Bacc("TRN2", target_bir_lowering=False, num_devices=1)
    args = [nc.dram_tensor(k, v.shape, mybir.dt.from_np(v.dtype), kind="ExternalInput").ap() for k, v in arrays.items()]
    outs = {
        "yT": (P, KT, TOK), "p_h": (DEPTH, 4, P, P), "p_g": (DEPTH, 2, P, P), "p_c": (DEPTH, 4, P, P),
        "p_n": (DEPTH, 4, P), "s_h": (DEPTH, DEC_B, 4, P, P),
        "s_g": (DEPTH, DEC_B, 2, P, P), "s_c": (DEPTH, DEC_B, 4, P, P), "s_n": (DEPTH, SMP, P),
        "s_m": (DEPTH, 4, 1 + DEC_B),
    }
    args += [nc.dram_tensor(k, s, F32, kind="ExternalOutput").ap() for k, s in outs.items()]
    args.append(nc.dram_tensor("x_keep", (P, KT, TOK), F32, kind="Internal").ap())
    build(nc, *args)
    r = run_bass_kernel_spmd(nc, [arrays], core_ids=[0]).results[0]
    y = r["yT"].transpose(2, 1, 0).reshape(TOK, D_MODEL)
    return (y[0:SEQ].reshape(1, SEQ, D_MODEL), y[SEQ:].reshape(DEC_B, DEC_T, D_MODEL),
            r["p_h"].reshape(DEPTH, 1, 4, P, P), r["p_g"].reshape(DEPTH, 1, 4, 64, P),
            r["p_c"].reshape(DEPTH, 1, 4, P, P), r["p_n"].reshape(DEPTH, 1, 4, P),
            r["s_m"][:, :, 0].reshape(DEPTH, 1, 4), r["s_h"], r["s_g"].reshape(DEPTH, DEC_B, 4, 64, P), r["s_c"],
            r["s_n"].reshape(DEPTH, DEC_B, 4, P),
            r["s_m"][:, :, 1:].transpose(0, 2, 1))
```

```python
import numpy as np
from contextlib import ExitStack

import concourse.bass as bass
from concourse import mybir

F32, F32R, U8 = mybir.dt.float32, mybir.dt.float32r, mybir.dt.uint8
ALU = mybir.AluOpType
ACT = mybir.ActivationFunctionType

P = 128
D_MODEL, D_FF, DEPTH = 1024, 2816, 2
SEQ, DEC_B, DEC_T = 512, 8, 4
SMP = DEC_B * DEC_T
TOK = SEQ + SMP
HALF = TOK // 2
KT = D_MODEL // P
HEADS, CH = 4, 128
NCH = SEQ // CH
LEVELS = 7
S_LEVELS = 2
EPS = 1e-6

FF_BLOCK = 8
FF_TILES = D_FF // P
FF_LAST = FF_TILES - 2 * FF_BLOCK
FFN_TILES = 2 * FF_TILES + 3 * KT

HQ, HF, HI, HG, SMALL, GQ, GK, GV, GG = 0, 4, 8, 12, 16, 17, 19, 21, 25
MIX_TILES = 102
MIX_PIECES = 90
MIX_T0 = MIX_P0 = FFN_TILES
FFN2_T0, FFN2_P0 = MIX_T0 + MIX_TILES, MIX_P0 + MIX_PIECES
TILES, PIECES = FFN2_T0 + FFN_TILES, FFN2_P0 + FFN_TILES
G0, B0, ML, G1, B1, G2, B2, WO = (29, 29), (37, 37), (45, 41), (61, 57), (69, 65), (77, 69), (85, 77), (93, 81)
ONE = 1
RING = 2
RAW = 2
assert TILES % 2 == 0 and PIECES % 2 == 0 and RING == RAW == 2

PG = {"next ffn1": 0, "mix": 8, "ffn2": 16}
P_HN, P_BG, P_BI, P_BF, P_LR = 24, 27, 29, 30, 31
NPAR = P_LR + 256
C_ID, C_DIAG, C_NEG = 0, 128, 256
C_NEGS = C_NEG + 128
C_SEL = C_NEGS + 32
C_BM = C_SEL + 512
NCONST = C_BM + 8

def scan_steps(br):
    if br < 2:
        s = [(("v", br, 0), 2), (("v", br, 1), 2), (("d", br, 0), 2), (("d", br, 1), 4)]
        s += [(("lv", br, l), 7) for l in range(1, LEVELS + 1)]
        s += [(("k", br, 0), 3), (("k", br, 1), 1), (("u", br, 0), 7)]
    else:
        s = [(("v", br, 0), 2), (("v", br, 1), 2)] + [(("a", br, h), 6) for h in range(HEADS)]
        s += [(("k", br, 0), 7), (("k", br, 1), 2), (("u", br, 0), 7), (("un", br, 0), 5), (("ns", br, 0), 1)]
    for h in range(HEADS):
        s += [(("m", br, h), 3)] if br == 2 else []
        s += [(("o", br, h), 8 if br == 2 else 4), (("z", br, h), 8)]
    return s


def weave(tiles, steps, keep=2):
    out, n, spent = [], 0, 0
    parts = []
    for t in tiles:
        parts += [("part", t[1], 0), ("tile", t[1], 1)] if t[0] == "tile" else [t]
    total = sum(w for _, w in steps)
    for s, w in steps:
        out.append(s)
        spent += w
        upto = round(spent * (len(parts) - keep) / total)
        out += parts[n:upto]
        n = upto
    return out + parts[n:]


def mixer_order():
    def group(t0, t1):
        return [("tile", t, 0) for t in range(t0, t1)]

    def branch(b):
        return [("branch", b, m) for m in range(KT)]

    scan0 = scan_steps(0)
    return (group(0, HG) + weave(group(HG, SMALL + 1), scan0[:6], 0)
            + [("rows", 0, 0), ("stab", 0, 0)] + group(GQ, GV) + [("exps", 0, 0), ("cols", 0, 0)]
            + weave(group(GV, G0[0]) + group(G0[0], B0[0]), scan0[6:])
            + weave(branch(0) + group(ML[0], G1[0]), scan_steps(1))
            + weave(group(G1[0], B1[0]) + branch(1) + group(G2[0], B2[0]), scan_steps(2), 4)
            + branch(2) + [("out", 0, 0)])


ORDER = mixer_order()
ONE_SIDED = ("tile", "part", "branch", "out", "stab", "exps")
STEP_NO = {s: i for i, s in enumerate([s for s in ORDER if s[0] not in ONE_SIDED])}
NSTEPS = len(STEP_NO)


def piece_of(t):
    for t0, p0 in (WO, G2, G1, ML):
        if t >= t0:
            return p0 + t - t0
    return t


class Chain:

    def __init__(self, eng, sem):
        self.eng, self.sem, self.base, self.n = eng, sem, ONE, 0

    def did(self, ins):
        ins.then_inc(self.sem, 1)
        self.n += 1

    def sync(self):
        self.eng.wait_ge(self.sem, self.base + self.n)

    def link(self, ins):
        self.did(ins)
        self.sync()

    def loop(self, reg, per):
        outer = Chain(self.eng, self.sem)
        outer.base, outer.n = self.base, self.n
        self.base, self.n = self.base + self.n + reg * per, 0
        return outer

    def end(self, outer, per, times):
        self.sync()
        assert self.n <= per, self.n
        if self.n < per:
            self.eng.sem_inc(self.sem, per - self.n)
        self.base, self.n = outer.base, outer.n + per * times


def build(nc, wst, xT, par_d, lb_d, const_d, lvm_d, fg_d, st_h, st_g, st_c, st_n, st_m,
          yT, p_h, p_g, p_c, p_n, s_h, s_g, s_c, s_n, s_m, x_keep):
    ctx = ExitStack()
    with ctx:
        top = [(nc.sbuf_base + 31) // 32 * 32]

        def sb(name, shape, dt=F32, at=None):
            size = 1 if dt == U8 else 4
            for d in shape[1:]:
                size *= d
            if at is None:
                at = top[0]
                top[0] += (size + 31) // 32 * 32
            return nc.alloc_sbuf_tensor_at(name, shape, dt, offset=at), at

        X, _ = sb("X", [P, KT, TOK])
        Hh, _ = sb("Hh", [P, KT, TOK], F32R)
        Hl, _ = sb("Hl", [P, KT, TOK], F32R)
        raw, _ = sb("raw", [P, RAW, 1024])
        Wh, _ = sb("Wh", [P, RING, 1024], F32R)
        Wl, _ = sb("Wl", [P, RING, 1024], F32R)
        const, _ = sb("const", [P, NCONST])
        ones, _ = sb("ones", [P, P])
        par, _ = sb("par", [P, NPAR])
        parL, _ = sb("parL", [P, DEPTH, 31])
        lvm, _ = sb("lvm", [P, LEVELS * P], U8)
        lbs, _ = sb("lbs", [P, DEPTH, 4])
        lbc, _ = sb("lbc", [P, 8])
        lbt, _ = sb("lbt", [P, 24])
        fg, _ = sb("fg", [P, KT])
        epsc, _ = sb("epsc", [P, 1])
        tmp, tmp_at = sb("tmp", [P, 6, TOK])
        vblk, _ = sb("vblk", [SMP, 1024], at=tmp_at + 3 * TOK * 4)
        dec, _ = sb("dec", [P, HEADS, NCH])
        decs, _ = sb("decs", [P, HEADS, DEC_B])
        wrow, _ = sb("wrow", [P, TOK])
        colG, _ = sb("colG", [P, 16])
        colW, _ = sb("colW", [P, 16])
        colS, _ = sb("colS", [SMP, 8])
        nst, nst_at = sb("nst", [SMP + HEADS, P])
        nS, _ = sb("nS", [P, SMP])
        nP, _ = sb("nP", [P, HEADS, NCH])
        nO, _ = sb("nO", [P, SMP + HEADS])
        nOt, _ = sb("nOt", [SMP + HEADS, P], at=nst_at)
        m0, _ = sb("m0", [HEADS, DEC_B])
        mO, _ = sb("mO", [HEADS, 1 + DEC_B])
        mch, _ = sb("mch", [HEADS, 1 + NCH])
        arena = top[0]
        setA, a_at = sb("setA", [P, 16, TOK])
        setB, b_at = sb("setB", [P, 16, TOK])
        kbuf, _ = sb("kbuf", [P, 4, TOK])
        att, att_at = sb("att", [P, 4, TOK])
        vts, _ = sb("vts", [SMP, 4, P])
        kts, _ = sb("kts", [SMP, 4, P])
        sst = [sb("sst0", [P, DEC_B, P])[0], sb("sst1", [P, DEC_B, P], at=tmp_at)[0]]
        gates, gates_at = sb("gates", [P, KT, TOK])
        rows, _ = sb("rows", [P, 6, TOK], at=gates_at)
        glr, _ = sb("glr", [16, TOK], at=gates_at + 6 * TOK * 4)
        oh = [sb("ohA", [P, 4, TOK], F32R, a_at)[0], sb("ohB", [P, 4, TOK], F32R, b_at)[0]]
        olo = [sb("olA", [P, 4, TOK], F32R, a_at + 8 * TOK * 4)[0], sb("olB", [P, 4, TOK], F32R, b_at + 8 * TOK * 4)[0]]
        Ah, f1 = sb("Ah", [P, FF_BLOCK, TOK], F32R, arena)
        Al, f2 = sb("Al", [P, FF_BLOCK, TOK], F32R, arena + FF_BLOCK * TOK * 4)
        Mh, _ = sb("Mh", [P, KT, TOK], F32R, b_at)
        Ml, _ = sb("Ml", [P, KT, TOK], F32R, b_at + KT * TOK * 4)

        SETS = [setA, setB, setA]
        R0 = [s[:, 0:4, :] for s in SETS]
        R1 = [s[:, 4:8, :] for s in SETS]
        R2 = [s[:, 8:12, :] for s in SETS]
        R3 = [s[:, 12:16, :] for s in SETS]
        KB = [kbuf[:, :, :], R1[1][:, 2:4, :], R1[2]]
        KTOK = [R1[0], R1[1][:, 0:2, :], kbuf[:, :, :]]
        OB = [R1[0], kbuf[:, :, :], kbuf[:, :, :]]
        OH = [oh[0], oh[1], oh[0]]
        OL = [olo[0], olo[1], olo[0]]

        dps = [ctx.enter_context(nc.psum_tensor(f"dense{i}", [P, 2, 512], F32)) for i in range(2)]
        SA = ctx.enter_context(nc.psum_tensor("SA", [P, 2, 512], F32))
        SB = ctx.enter_context(nc.psum_tensor("SB", [P, 2, 512], F32))

        def sem(name):
            return ctx.enter_context(nc.semaphore(name))

        raw_in = [sem(f"raw_in{i}") for i in range(RAW)]
        raw_free = sem("raw_free")
        w_ready = sem("w_ready")
        w_used = sem("w_used")
        tile_done = sem("tile_done")
        slot_free = [sem(f"slot_free{i}") for i in range(2)]
        consts_in = sem("consts_in")
        par_in = sem("par_in")
        x_in = [sem(f"x_in{i}") for i in range(4)]
        silu_done, ffn_prod = sem("silu_done"), sem("ffn_prod")
        dlink, alink, glink = sem("dlink"), sem("alink"), sem("glink")
        const_ready = sem("const_ready")
        ssq_ready, rms_sum, rs_ready = sem("ssq_ready"), sem("rms_sum"), sem("rs_ready")
        norm_h, norm_hi, norm_lo = sem("norm_h"), sem("norm_hi"), sem("norm_lo")
        ffn_hi, ffn_lo = sem("ffn_hi"), sem("ffn_lo")
        sig_done = sem("sig_done")
        x_read = sem("x_read")
        la_1, la_2, la_3 = sem("la_1"), sem("la_2"), sem("la_3")
        lr_used = sem("lr_used")
        pe_step, dve_step, act_step = sem("pe_step"), sem("dve_step"), sem("act_step")
        step_began = sem("step_began")
        split_began = sem("split_began")
        dve_began = sem("dve_began")
        row_x = sem("row_x")
        row_y = sem("row_y")
        row_e = sem("row_e")
        st_upd = sem("st_upd")
        m_in = sem("m_in")
        st_in = [sem("st_in0"), sem("st_in1")]
        st_out = [sem("st_out0"), sem("st_out1")]
        st_mem = sem("st_mem")
        d_exp, e_exp, d_abs = sem("d_exp"), sem("e_exp"), sem("d_abs")
        h_rs, h_of, h_hi, h_lo = sem("h_rs"), sem("h_of"), sem("h_hi"), sem("h_lo")
        br_sig = sem("br_sig")
        mg_f, mg_hi, mg_lo = sem("mg_f"), sem("mg_hi"), sem("mg_lo")
        x_back = sem("x_back")
        y_ready, y_out = sem("y_ready"), sem("y_out")
        out_sem = sem("out_sem")

        ident = const[:, C_ID:C_ID + 128]
        diag = const[:, C_DIAG:C_DIAG + 128]

        def mask(l):
            return lvm[:, (l - 1) * P:l * P]

        def halves(ap):
            return ap.rearrange("p (a b) -> p a b", a=2)

        def f32(ap):
            return ap.bitcast(F32)

        def kt(br, h):
            return h // 2 if br == 1 else h

        def st_no(br, h):
            return h if br == 0 else 4 + h // 2 if br == 1 else 6 + h

        block = ctx.enter_context(nc.Block())

        @block.sync
        def _(sp):
            sp.sem_inc(raw_free, RAW)
            with sp.Fori(0, DEPTH * PIECES // 2) as it:
                for j in range(2):
                    sp.wait_ge(raw_free, it * 2 + (j + 1))
                    sp.dma_start(raw[:, j, :], wst[it * 2 + j, :, :]).then_inc(raw_in[j], 16)

        @block.gpsimd
        def _(pool):
            pool.sem_inc(w_used, RING - 1)
            with pool.Fori(0, DEPTH * PIECES // 2) as it:
                for j in range(2):
                    pool.wait_ge(raw_in[j], it * 16 + 16)
                    pool.wait_ge(w_used, it * 2 + (j + 1))
                    pool.sem_inc(split_began, 1)
                    pool.tensor_scalar(Wh[:, j, :], raw[:, j, :], 1.0, 0.0, ALU.mult, ALU.add).then_inc(glink, 1)
                    pool.wait_ge(glink, it * 4 + (2 * j + 1))
                    pool.tensor_tensor(Wl[:, j, :], raw[:, j, :], f32(Wh[:, j, :]), ALU.subtract).then_inc(glink, 1)
                    pool.wait_ge(glink, it * 4 + (2 * j + 2))
                    pool.sem_inc(w_ready, 1)
                    pool.sem_inc(raw_free, 1)

        @block.tensor
        def _(pe):
            def dense(p, t, ring, slot, use, hi, lo, k0, nk, first=None, part=None):
                if part != 1:
                    pe.wait_ge(w_ready, p + 1)
                    pe.wait_ge(slot_free[slot], ONE + use)
                for k in range(nk) if part is None else range(part * nk // 2, (part + 1) * nk // 2):
                    if first is not None:
                        pe.wait_ge(first[0], first[1] + (k + 1))
                    w0 = (k0 + k) * 128
                    for n, (w, x) in enumerate(((Wh, hi), (Wh, lo), (Wl, hi))):
                        for a in range(2):
                            mm = pe.matmul(dps[slot][:, a, 0:HALF], w[:, ring, w0:w0 + 128],
                                           x[:, k, a * HALF:(a + 1) * HALF],
                                           start=(k == 0 and n == 0), stop=(k == nk - 1 and n == 2))
                    if k == 0 and k0 == 0:
                        pe.wait_ge(tile_done, ONE + t)
                        pe.sem_inc(w_used, 1)
                if part != 0:
                    mm.then_inc(tile_done, 1)

            def rms(n):
                pe.wait_ge(ssq_ready, n + 1)
                for a in range(2):
                    mm = pe.matmul(SB[:, a, 0:HALF], ones[:, :], tmp[:, 3, a * HALF:(a + 1) * HALF],
                                   start=True, stop=True)
                mm.then_inc(rms_sum, 1)

            def ffn(L, t0, p0, norm_no, which):
                hi, lo = ((Hh, Hl), (Mh, Ml))[which]

                def up(off, j, i, first=None):
                    u = L * (TILES // 2) + (t0 + off) // 2 + i * 2 + j // 2
                    dense(L * PIECES + (p0 + off + j) + i * 4, L * TILES + (t0 + off + j) + i * 4,
                          j % RING, j % 2, u, hi, lo, 0, KT, first)

                for b, nf in enumerate((FF_BLOCK, FF_BLOCK, FF_LAST)):
                    off = b * 24
                    if b == 0:
                        for j in range(4):
                            up(off, j, 0, (norm_lo, norm_no * KT) if j == 0 else None)
                            if j == 0:
                                rms(norm_no)
                    with pe.Fori(1 if b == 0 else 0, nf // 2) as i:
                        for j in range(4):
                            up(off, j, i)
                    hidden = L * (2 * FF_TILES) + (which * FF_TILES + b * FF_BLOCK)
                    with pe.Fori(0, 2) as i:
                        for j in range(4):
                            u = L * (TILES // 2) + (t0 + off + 2 * nf) // 2 + i * 2 + j // 2
                            dense(L * PIECES + (p0 + off + 2 * nf + j) + i * 4,
                                  L * TILES + (t0 + off + 2 * nf + j) + i * 4, j % RING, j % 2, u,
                                  Ah, Al, 0, nf, (ffn_lo, hidden) if j == 0 else None)

            def tile(L, t, hi, lo, nk=KT, p=None, k0=0, first=None, part=None):
                g = MIX_T0 + t
                p = piece_of(t) if p is None else p
                dense(L * PIECES + (MIX_P0 + p), L * TILES + g, (MIX_P0 + p) % RING, g % 2, L * (TILES // 2) + g // 2,
                      hi, lo, k0, nk, first, part)

            def sample_products(br):
                for hh in range(HEADS):
                    mm = pe.matmul(SB[0:SMP, 0, hh * SMP:(hh + 1) * SMP], KB[br][:, kt(br, hh), SEQ:TOK],
                                   R0[br][:, hh, SEQ:TOK], start=True, stop=True)
                return mm

            def tpose(out, in_, idn):
                return pe.transpose(out, in_, idn)

            def step(L, s):
                kind, br, h = s
                no = L * NSTEPS + STEP_NO[s]
                pe.wait_ge(dve_step, ONE + no)
                pe.wait_ge(act_step, ONE + no)
                pe.sem_inc(step_began, 1)
                mm = None
                Q, K, V = R0[br], KB[br], R2[br]
                Tk, att_ = KTOK[br], att
                if kind == "rows":
                    pe.wait_ge(lr_used, L * 2 + 1)
                    for i in range(2):
                        for a in range(2):
                            bank = (SA, SB)[i]
                            mm = pe.matmul(bank[:, a, 0:HALF], par[0:16, P_LR + i * 128:P_LR + (i + 1) * 128],
                                           glr[:, a * HALF:(a + 1) * HALF], start=True, stop=True)
                elif kind == "cols":
                    pe.wait_ge(row_x, L + 1)
                    pe.wait_ge(row_e, L + 1)
                    pe.sem_inc(step_began, 1)
                    for r, c0 in ((4, 0), (5, 32)):
                        for c in range(NCH):
                            tpose(SA[:, 0, c0 + c * 4:c0 + c * 4 + 4], rows[0:4, r, c * CH:(c + 1) * CH],
                                  ident[0:4, 0:4])
                        tpose(SA[0:SMP, 1, c0:c0 + 4], rows[0:4, r, SEQ:TOK], ident[0:4, 0:4])
                    pe.wait_ge(m_in, L * 32 + 32)
                    pe.sem_inc(step_began, 1)
                    mm = tpose(SB[:, 0, 0:SMP], nst[0:SMP, :], ident[0:SMP, 0:SMP])
                elif kind == "v":
                    for i in range(2):
                        for c in range(NCH):
                            tpose(SA[:, i, c * CH:(c + 1) * CH], V[:, 2 * h + i, c * CH:(c + 1) * CH], ident)
                        mm = tpose(SB[0:SMP, 0, i * P:(i + 1) * P], V[:, 2 * h + i, SEQ:TOK], ident)
                elif kind == "d":
                    for i in range(2):
                        hh = 2 * h + i
                        for c in range(NCH):
                            cs = slice(c * CH, (c + 1) * CH)
                            mm = pe.matmul(SA[:, i, cs], K[:, kt(br, hh), cs], Q[:, hh, cs], start=True, stop=True)
                    if h == 0:
                        mm = sample_products(br)
                elif kind == "lv":
                    bs, hf = 1 << h, 1 << (h - 1)
                    for hh in range(0, HEADS, 2 if br == 1 else 1):
                        for c in range(NCH):
                            col = (hh % 2) * 256 + c * 64
                            if br == 1:
                                qs = Q[:, hh:hh + 2, c * CH:(c + 1) * CH].rearrange("p h (n b) -> p h n b", b=bs)
                                o = SA[:, hh // 2, :].rearrange("p (h n) -> p h n", h=2)
                                for s0 in range(0, CH, bs) if hf >= 32 else (0,):
                                    e, n = (s0 + hf, 1) if hf >= 32 else (CH, CH // bs)
                                    o0 = c * 64 + s0 // bs * hf
                                    mm = pe.matmul(o[s0:e, :, o0:o0 + n * hf].rearrange("p h (n b) -> p h n b", b=hf),
                                                   K[:, kt(br, hh), c * CH + s0:c * CH + e],
                                                   qs[:, :, s0 // bs:s0 // bs + n, hf:bs], start=True, stop=True)
                                continue
                            if hf >= 32:
                                for s0 in range(0, CH, bs):
                                    o0 = col + s0 // bs * hf
                                    mm = pe.matmul(SA[s0:s0 + hf, hh // 2, o0:o0 + hf],
                                                   K[:, kt(br, hh), c * CH + s0:c * CH + s0 + hf],
                                                   Q[:, hh, c * CH + s0 + hf:c * CH + s0 + bs],
                                                   start=True, stop=True)
                                continue
                            q = Q[:, hh, c * CH:(c + 1) * CH].rearrange("p (n b) -> p n b", b=bs)[:, :, hf:bs]
                            mm = pe.matmul(SA[:, hh // 2, col:col + 64], K[:, kt(br, hh), c * CH:(c + 1) * CH],
                                           q, start=True, stop=True)
                    if h <= S_LEVELS:
                        mm = sample_products(br)
                elif kind == "a":
                    for c in range(NCH):
                        cs = slice(c * CH, (c + 1) * CH)
                        pe.matmul(SA[:, 1, cs], K[:, h, cs], Q[:, h, cs], start=True, stop=True)
                    pe.matmul(SB[0:SMP, 0, 32:64], K[:, h, SEQ:TOK], Q[:, h, SEQ:TOK], start=True, stop=True)
                    s0, s1 = sel(0, h), sel(1, h)
                    pe.matmul(SA[:, 0, :], s0, wrow[0:4, 0:SEQ], start=True, stop=True)
                    pe.matmul(SB[0:SMP, 0, 0:32], s0[:, 0:SMP], wrow[0:4, SEQ:TOK], start=True, stop=True)
                    pe.matmul(SB[:, 1, :], s1, wrow[32:36, 0:SEQ], start=True, stop=True)
                    mm = pe.matmul(SB[:, 0, 64:96], s1, wrow[32:36, SEQ:TOK], start=True, stop=True)
                elif kind == "k":
                    nt = 2 if br == 1 else 4
                    for i in range(nt):
                        if h == 0:
                            for c in range(NCH):
                                mm = tpose((SA, SB)[i // 2][:, i % 2, c * CH:(c + 1) * CH],
                                           K[:, i, c * CH:(c + 1) * CH], ident)
                        else:
                            mm = tpose(SA[0:SMP, 0, i * P:(i + 1) * P], K[:, i, SEQ:TOK], ident)
                elif kind == "u":
                    for hh in range(HEADS):
                        for c in range(NCH):
                            cs = slice(c * CH, (c + 1) * CH)
                            if br == 1:
                                e = 64 * (hh % 2)
                                mm = pe.matmul(SA[e:e + 64, hh // 2, cs], Tk[:, hh // 2, c * CH + e:c * CH + e + 64],
                                               V[:, hh, cs], start=True, stop=True)
                            else:
                                mm = pe.matmul((SA, SB)[hh // 2][:, hh % 2, cs], Tk[:, hh, cs], V[:, hh, cs],
                                               start=True, stop=True)
                elif kind == "un":
                    for hh in range(HEADS):
                        for c in range(NCH):
                            pe.matmul(SA[:, 0, hh * 4 + c:hh * 4 + c + 1], Tk[:, hh, c * CH:(c + 1) * CH],
                                      ones[:, 0:1], start=True, stop=True)
                        mm = pe.matmul(SA[:, 0, 64 + hh * 8:72 + hh * 8], kts[:, hh, :],
                                       const[0:SMP, C_BM:C_BM + 8], start=True, stop=True)
                elif kind == "ns":
                    mm = tpose(SA[0:SMP + HEADS, 0, 0:P], nO[:, :], ident)
                elif kind == "m":
                    pe.matmul(SA[:, 0, :], sel(2, h), wrow[64:68, 0:SEQ], start=True, stop=True)
                    mm = pe.matmul(SA[:, 1, 0:SMP], sel(2, h), wrow[64:68, SEQ:TOK], start=True, stop=True)
                elif kind == "o":
                    n = st_no(br, h)
                    pe.wait_ge(st_in[n % 2], L * 80 + 16 * (n // 2 + 1))
                    pe.sem_inc(step_began, 1)
                    for c in range(NCH):
                        cs = slice(c * CH, (c + 1) * CH)
                        pe.matmul(SA[:, 0, cs], V[:, h, cs], att[:, h, cs], start=True, stop=(c == 0))
                        if c:
                            ps = slice((c - 1) * CH, c * CH)
                            pe.matmul(SA[:, 0, cs], K[:, kt(br, h), ps], Q[:, h, cs], start=False, stop=True)
                    if br == 2:
                        pe.matmul(SB[:, 0, 0:CH], ones[:, :], att[:, h, 0:CH], start=True, stop=True)
                        pe.matmul(SB[:, 0, CH:SEQ], ones[:, :], att[:, h, CH:SEQ], start=True, stop=False)
                        pe.matmul(SB[:, 0, CH:SEQ], ones[:, :], tmp[:, 5, CH:SEQ], start=False, stop=True)
                        pe.matmul(SB[:, 1, 0:SMP], ones[0:SMP, :], att[0:SMP, h, SEQ:TOK], start=True, stop=False)
                        pe.matmul(SB[:, 1, 0:SMP], ones[:, :], tmp[:, 5, SEQ:TOK], start=False, stop=True)
                    pe.matmul(SA[:, 1, 0:SMP], vts[:, h, :], att[0:SMP, h, SEQ:TOK], start=True, stop=False,
                              skip_group_check=True)
                    for b in range(DEC_B):
                        mm = pe.matmul(SA[:, 1, b * DEC_T:(b + 1) * DEC_T], sst[n % 2][:, b, :],
                                       Q[:, h, SEQ + b * DEC_T:SEQ + (b + 1) * DEC_T],
                                       start=False, stop=(b == DEC_B - 1), skip_group_check=True)
                elif kind == "z":
                    for i in range(2):
                        if br == 1:
                            e = 64 * (h % 2)
                            mm = pe.matmul(SB[e:e + 64, i, :], kts[:, h // 2, e:e + 64],
                                           vblk[:, i * 512:(i + 1) * 512], start=True, stop=True)
                        else:
                            mm = pe.matmul(SB[:, i, :], kts[:, h, :], vblk[:, i * 512:(i + 1) * 512],
                                           start=True, stop=True)
                    for a in range(2):
                        mm = pe.matmul(SA[:, a, 0:HALF], ones[:, :], tmp[:, 2, a * HALF:(a + 1) * HALF],
                                       start=True, stop=True)
                mm.then_inc(pe_step, 1)

            def sel(q, h):
                return const[32 * q:32 * q + 4, C_SEL + h * 128:C_SEL + (h + 1) * 128]

            pe.sem_inc(tile_done, ONE)
            pe.sem_inc(pe_step, ONE)
            with pe.Fori(0, DEPTH) as L:
                ffn(L, 0, 0, L * 3, 0)
                rms(L * 3 + 1)
                for s in ORDER:
                    what, n, m = s
                    if what == "part":
                        tile(L, n, Hh, Hl, part=0)
                    elif what == "tile":
                        tile(L, n, Hh, Hl, first=(norm_lo, (L * 3 + 1) * KT) if n == 0 else None,
                             part=1 if m else None)
                    elif what == "branch":
                        t0, p0 = (B0, B1, B2)[n]
                        tile(L, t0 + m, OH[n], OL[n], 4, p0 + m // 2, 4 * (m % 2),
                             first=(h_lo, L * 12 + n * 4) if m == 0 else None)
                    elif what not in ONE_SIDED:
                        step(L, s)
                for m in range(KT):
                    tile(L, WO[0] + m, Hh, Hl, first=(mg_lo, L * KT) if m == 0 else None)
                pe.wait_ge(tile_done, ONE + L * TILES + (FFN2_T0 - 1))
                pe.sem_inc(w_used, 1)
                pe.sem_inc(tile_done, 1)
                ffn(L, FFN2_T0, FFN2_P0, L * 3 + 2, 1)
            rms(3 * DEPTH)

        @block.scalar
        def _(act):
            ch = Chain(act, alink)
            act.sem_inc(alink, ONE)
            act.sem_inc(act_step, ONE)
            act.sem_inc(slot_free[0], ONE)

            def act_norm(n, L=None):
                act.wait_ge(rms_sum, n + 1)
                ch.sync()
                ch.link(act.activation(halves(tmp[:, 2, :]), SB[:, :, 0:HALF], ACT.Ln, bias=epsc[:, :],
                                       scale=1.0 / D_MODEL))
                act.activation(tmp[:, 2, :], tmp[:, 2, :], ACT.Exp, scale=-0.5).then_inc(rs_ready, 1)
                if L is None:
                    return
                for k in range(KT):
                    act.wait_ge(norm_h, L * KT + (k + 1))
                    act.activation(Hh[:, k, :], tmp[:, k % 2, :], ACT.Copy).then_inc(norm_hi, 1)

            def ffn(L, t0, norm_no, which):
                act_norm(norm_no)
                for b, nf in enumerate((FF_BLOCK, FF_BLOCK, FF_LAST)):
                    off = b * 24
                    with act.Fori(0, nf // 2) as i:
                        for j in range(2):
                            f = L * (2 * FF_TILES) + (which * FF_TILES + b * FF_BLOCK + j) + i * 2
                            use = L * (TILES // 2) + ((t0 + off) // 2 + j + 1) + i * 2
                            act.wait_ge(slot_free[0], ONE + use)
                            act.activation(tmp[:, 4 + j, :], tmp[:, 4 + j, :], ACT.Silu).then_inc(silu_done, 1)
                            act.wait_ge(ffn_prod, f + 1)
                            act.activation(Ah[:, bass.ds(i * 2 + j, 1), :], tmp[:, j:j + 1, :],
                                           ACT.Copy).then_inc(ffn_hi, 1)
                if which:
                    for m in range(KT):
                        use = L * (TILES // 2) + (t0 + off + 2 * nf + m) // 2 + 1
                        scaled_hi(Hh, m, 0, m % 2, use)

            def scaled_hi(dst, m, g0, slot, use):
                act.wait_ge(slot_free[slot], ONE + use)
                act.activation(dst[:, m, :], X[:, m, :], ACT.Copy,
                               scale=par[:, g0 + m:g0 + m + 1]).then_inc(norm_hi, 1)

            def tile_wait(L, t):
                act.wait_ge(tile_done, ONE + L * TILES + (MIX_T0 + t + 1))

            def tile(L, t):
                slot = (MIX_T0 + t) % 2
                ps = dps[slot][:, :, 0:HALF]
                free = slot_free[slot]
                if t in range(HQ, HF) or t in range(HG, SMALL) or t in range(GG, G0[0]):
                    tile_wait(L, t)
                    act.wait_ge(free, ONE + L * (TILES // 2) + (MIX_T0 + t) // 2)
                    act.activation(halves(tmp[:, t % 2, :]), ps, ACT.Sigmoid).then_inc(sig_done, 1)
                elif t in range(HF, HI):
                    tile_wait(L, t)
                    act.activation(halves(R1[0][:, t - HF, :]), ps, ACT.Sigmoid).then_inc(sig_done, 1)
                    act.activation(halves(kbuf[:, t - HF, :]), ps, ACT.Sigmoid, scale=-1.0).then_inc(free, 1)
                elif t in range(GQ, GK):
                    tile_wait(L, t)
                    for e in range(2):
                        ins = act.activation(halves(R0[1][64 * e:64 * e + 64, 2 * (t - GQ) + e, :]),
                                             dps[slot][64 * e:64 * e + 64, :, 0:HALF], ACT.Copy, scale=0.125)
                        ch.did(ins)
                    ch.sync()
                    act.sem_inc(free, 1)
                elif t in range(HI, HG) or t in range(GK, GG) or t in range(ML[0], ML[0] + 12):
                    tile_wait(L, t)
                    scale = 1.0
                    if t < HG:
                        dst = R2[0][:, t - HI, :]
                    elif t < GV:
                        dst = R1[1][:, 2 + t - GK, :]
                    elif t < GG:
                        dst = R2[1][:, t - GV, :]
                    else:
                        u = t - ML[0]
                        dst = (R0, R1, R2)[u // 4][2][:, u % 4, :]
                        if u // 4 == 1:
                            scale = float(P) ** -0.5
                    act.activation(halves(dst), ps, ACT.Copy, scale=scale).then_inc(free, 1)
                elif t in range(ML[0] + 12, G1[0]):
                    tile_wait(L, t)
                    act.activation(halves(R3[2][:, t - ML[0] - 12, :]), ps, ACT.Sigmoid).then_inc(free, 1)
                elif t >= G0[0]:
                    m = [t - g[0] for g in (G0, G1, G2) if 0 <= t - g[0] < KT][0]
                    tile_wait(L, t)
                    act.activation(halves(gates[:, m, :]), ps, ACT.Sigmoid).then_inc(free, 1)

            def dma_state(L, i, store):
                if i < 4:
                    d, v = (s_h, st_h), (lambda a: a[L, :, i, :, :].rearrange("b d v -> d b v"))
                elif i < 6:
                    d, v = (s_g, st_g), (lambda a: a[L, :, i - 4, :, :].rearrange("b d v -> d b v"))
                else:
                    d, v = (s_c, st_c), (lambda a: a[L, :, i - 6, :, :].rearrange("b d v -> d b v"))
                if store:
                    act.dma_start(v(d[0]), sst[i % 2][:, :, :]).then_inc(st_out[i % 2], 16)
                else:
                    act.dma_start(sst[i % 2][:, :, :], v(d[1])).then_inc(st_in[i % 2], 16)

            def exps(L):
                act.wait_ge(row_x, L + 1)
                ch.did(act.activation(wrow[32:36, :], rows[0:4, 1, :], ACT.Exp))
                ch.did(act.activation(wrow[64:68, :], rows[0:4, 3, :], ACT.Exp, scale=-1.0))
                ch.link(act.activation(rows[0:4, 5, :], rows[0:4, 0, :], ACT.Exp))
                act.sem_inc(row_e, 1)

            def step(L, s):
                kind, br, h = s
                no = L * NSTEPS + STEP_NO[s]
                Q, K, V, Tk, O = R0[br], KB[br], R2[br], KTOK[br], OB[br]
                act.wait_ge(pe_step, ONE + no + 1)
                ch.sync()
                if kind == "rows":
                    act.wait_ge(la_1, L + 1)
                    for i in range(2):
                        ch.did(act.activation(halves(setB[:, 4 + i, :]), (SA, SB)[i][:, :, 0:HALF], ACT.Abs,
                                              bias=par[:, P_BG + i:P_BG + i + 1]))
                    ch.did(act.activation(rows[0:4, 2, :], rows[0:4, 1, :], ACT.Abs,
                                          bias=par[0:4, P_BF:P_BF + 1]))
                    ch.sync()
                    ch.link(act.activation(setB[:, 6:8, :], setB[:, 4:6, :], ACT.Exp, scale=-1.0))
                    act.activation(setB[:, 6:8, :], setB[:, 6:8, :], ACT.Ln, bias=1.0).then_inc(la_2, 1)
                    act.wait_ge(la_3, L * 1 + 1)
                    ch.did(act.activation(setB[:, 4:6, :], setB[:, 4:6, :], ACT.Exp, scale=1.0 / 16))
                    ch.link(act.activation(rows[0:4, 2, :], rows[0:4, 2, :], ACT.Exp, scale=-1.0))
                    act.activation(rows[0:4, 2, :], rows[0:4, 2, :], ACT.Ln, bias=1.0).then_inc(row_y, 1)
                elif kind == "v":
                    ch.did(act.activation(V[:, 2 * h:2 * h + 2, 0:SEQ], SA[:, :, :], ACT.Copy))
                    ch.did(act.activation(vts[:, 2 * h:2 * h + 2, :].rearrange("p a b -> p (a b)"),
                                          SB[0:SMP, 0, 0:2 * P], ACT.Copy))
                elif kind == "a":
                    act.wait_ge(d_exp, (L * HEADS + h) + 1)
                    act.activation(att[:, h, 0:SEQ], att[:, h, 0:SEQ], ACT.Exp).then_inc(e_exp, 1)
                    act.activation(att[0:SMP, h, SEQ:TOK], att[0:SMP, h, SEQ:TOK], ACT.Exp).then_inc(e_exp, 1)
                elif kind == "k":
                    nt = 2 if br == 1 else 4
                    if h == 0:
                        for i in range(nt):
                            src = (SA, SB)[i // 2]
                            if br == 2:
                                for c in range(NCH):
                                    cs = slice(c * CH, (c + 1) * CH)
                                    ch.did(act.activation(Tk[:, i, cs], src[:, i % 2, cs], ACT.Copy,
                                                          scale=colW[:, c * 4 + i:c * 4 + i + 1]))
                            elif i % 2 == 0:
                                ch.did(act.activation(Tk[:, i:i + 2, 0:SEQ], src[:, :, :], ACT.Copy))
                    elif br == 2:
                        for i in range(nt):
                            ch.did(act.activation(kts[:, i, :], SA[0:SMP, 0, i * P:(i + 1) * P], ACT.Copy,
                                                  scale=colS[:, 4 + i:5 + i]))
                    else:
                        ch.did(act.activation(kts[:, 0:nt, :].rearrange("p a b -> p (a b)"),
                                              SA[0:SMP, 0, 0:nt * P], ACT.Copy))
                elif kind == "ns":
                    ch.link(act.activation(nOt[:, :], SA[0:SMP + HEADS, 0, 0:P], ACT.Copy))
                    act.dma_start(s_n[L, :, :], nOt[0:SMP, :]).then_inc(out_sem, 16)
                    act.dma_start(p_n[L, :, :], nOt[SMP:SMP + HEADS, :]).then_inc(out_sem, 16)
                elif kind == "m":
                    ch.did(act.activation(tmp[:, 3, 0:SEQ], SA[:, 0, :], ACT.Copy))
                    ch.did(act.activation(tmp[:, 3, SEQ:TOK], SA[:, 1, 0:SMP], ACT.Copy))
                elif kind == "o":
                    if h == 0:
                        act.wait_ge(dve_step, ONE + L * NSTEPS + (STEP_NO[("u", br, 0)] + 1))
                        for i in range(2 if br == 1 else 4):
                            dst = (p_h, p_g, p_c)[br]
                            act.dma_start(dst[L, i, :, :], K[:, i, 3 * CH:4 * CH]).then_inc(out_sem, 16)
                    if br == 2:
                        act.activation(tmp[:, 5, 0:SEQ], SB[:, 0, :], ACT.Abs).then_inc(d_abs, 1)
                        act.activation(tmp[:, 5, SEQ:TOK], SB[:, 1, 0:SMP], ACT.Abs).then_inc(d_abs, 1)
                    if br < 2:
                        ch.did(act.activation(O[:, h, 0:SEQ], SA[:, 0, :], ACT.Copy))
                        ch.did(act.activation(O[:, h, SEQ:TOK], SA[:, 1, 0:SMP], ACT.Copy))
                        ch.did(act.activation(tmp[:, 2, 0:SEQ], SA[:, 0, :], ACT.Square))
                        ch.did(act.activation(tmp[:, 2, SEQ:TOK], SA[:, 1, 0:SMP], ACT.Square))
                    n = st_no(br, h)
                    if 0 < n < 9 and (br != 1 or h % 2 == 0):
                        act.wait_ge(st_out[(n - 1) % 2], L * 80 + 16 * ((n - 1) // 2 + 1))
                        dma_state(L, n + 1, False)
                elif kind == "z":
                    idx = L * 12 + (br * 4 + h)
                    ch.link(act.activation(halves(tmp[:, 5, :]), SA[:, :, 0:HALF], ACT.Ln, bias=epsc[:, :],
                                           scale=1.0 / P))
                    act.activation(tmp[:, 5, :], tmp[:, 5, :], ACT.Exp, scale=-0.5).then_inc(h_rs, 1)
                    act.wait_ge(h_of, idx + 1)
                    act.activation(OH[br][:, h, :], O[:, h, :], ACT.Copy).then_inc(h_hi, 1)
                    if br != 1 or h % 2 == 1:
                        act.wait_ge(st_upd, idx + 1)
                        dma_state(L, st_no(br, h), True)
                ch.sync()
                act.sem_inc(act_step, 1)

            act.dma_start(parL[:, :, :], par_d).then_inc(par_in, 16)
            for i in range(4):
                act.dma_start(X[:, 2 * i:2 * i + 2, :], xT[:, 2 * i:2 * i + 2, :]).then_inc(x_in[i], 16)
            act.dma_start(const[:, :], const_d).then_inc(consts_in, 16)
            act.dma_start(kbuf[:, 0:2, 0:448], lvm_d).then_inc(consts_in, 16)
            act.dma_start(lbt[:, 0:8], lb_d).then_inc(consts_in, 16)
            act.dma_start(fg[:, :], fg_d).then_inc(consts_in, 16)
            act.wait_ge(par_in, 16)
            for m in range(KT):
                act.wait_ge(x_in[m // 2], 16)
                act.activation(Hh[:, m, :], X[:, m, :], ACT.Copy,
                               scale=parL[:, DEPTH - 1, m:m + 1]).then_inc(norm_hi, 1)
            act.wait_ge(const_ready, 1)
            act.activation(lbt[:, 8:16], lbt[:, 8:16], ACT.Exp).then_inc(const_ready, 1)
            with act.Fori(0, DEPTH) as L:
                outer = ch.loop(L, 1024)
                ffn(L, 0, L * 3, 0)
                act_norm(L * 3 + 1, L)
                act.dma_start(x_keep, X[:, :, :]).then_inc(x_read, 16)
                act.dma_start(nst[0:SMP, :], st_n[L, :, :]).then_inc(m_in, 16)
                act.dma_start(m0[:, :], st_m[L, :, :]).then_inc(m_in, 16)
                dma_state(L, 0, False)
                for s in ORDER:
                    if s[0] == "tile":
                        tile(L, s[1])
                        if s[1] == G0[0]:
                            for g in (MIX_T0 + G0[0] - 2, MIX_T0 + G0[0] - 1):
                                act.wait_ge(slot_free[g % 2], ONE + L * (TILES // 2) + (g // 2 + 1))
                            dma_state(L, 1, False)
                    elif s[0] == "out":
                        act.dma_start(s_m[L, :, :], mO[:, :]).then_inc(out_sem, 16)
                        for m in range(KT):
                            act.wait_ge(mg_f, (L * KT + m) + 1)
                            act.activation(Hh[:, m, :], X[:, m, :], ACT.Copy).then_inc(mg_hi, 1)
                        act.wait_ge(mg_lo, (L + 1) * KT)
                        act.wait_ge(x_read, L * 32 + 16)
                        act.dma_start(X[:, :, :], x_keep).then_inc(x_read, 16)
                    elif s[0] == "exps":
                        exps(L)
                    elif s[0] not in ONE_SIDED:
                        step(L, s)
                act.wait_ge(out_sem, (L + 1) * (16 * 13))
                act.wait_ge(st_out[0], (L + 1) * 80)
                act.wait_ge(st_out[1], (L + 1) * 80)
                for m in range(KT):
                    g = MIX_T0 + WO[0] + m
                    scaled_hi(Mh, m, PG["ffn2"], g % 2, L * (TILES // 2) + (g // 2 + 1))
                ffn(L, FFN2_T0, L * 3 + 2, 1)
                ch.end(outer, 1024, DEPTH)
            act_norm(3 * DEPTH)
            for k in range(KT):
                act.wait_ge(y_ready, k + 1)
                act.dma_start(yT[:, k, :], X[:, k, :]).then_inc(y_out, 16)
            act.wait_ge(y_out, 16 * KT)

        @block.vector
        def _(dve):
            ch = Chain(dve, dlink)
            dve.sem_inc(dlink, ONE)
            dve.sem_inc(dve_step, ONE)
            dve.sem_inc(slot_free[1], ONE)
            TT, TS, STT = dve.tensor_tensor, dve.tensor_scalar, dve.scalar_tensor_tensor

            def square_sum(m):
                ch.sync()
                ch.link(TT(tmp[:, 4:5, :], X[:, m, :], X[:, m, :], ALU.mult))
                ch.did(TT(tmp[:, 3:4, :], tmp[:, 3:4, :], tmp[:, 4:5, :], ALU.add))

            def ssq_start():
                ch.did(dve.memset(tmp[:, 3, :], 0.0))

            def ssq_end():
                ch.sync()
                dve.sem_inc(ssq_ready, 1)

            def scaled_lo(dst, hi, m, g, n):
                dve.wait_ge(norm_hi, n * KT + (m + 1))
                STT(dst[:, m, :], X[:, m, :], g, f32(hi[:, m, :]), ALU.mult, ALU.subtract).then_inc(norm_lo, 1)

            def norm(n, g0):
                dve.wait_ge(rs_ready, n + 1)
                for k in range(KT + 1):
                    if k < KT:
                        if k > 1:
                            dve.wait_ge(norm_lo, n * KT + (k - 1))
                        STT(tmp[:, k % 2, :], X[:, k, :], par[:, g0 + k:g0 + k + 1], tmp[:, 2, :],
                            ALU.mult, ALU.mult).then_inc(norm_h, 1)
                    if k:
                        dve.wait_ge(norm_hi, n * KT + k)
                        TT(Hl[:, k - 1, :], tmp[:, (k - 1) % 2, :], f32(Hh[:, k - 1, :]),
                           ALU.subtract).then_inc(norm_lo, 1)

            def ffn(L, t0, norm_no, which):
                rs = halves(tmp[:, 2, :])
                dve.wait_ge(rs_ready, norm_no + 1)
                dve.sem_inc(dve_began, 1)
                for b, nf in enumerate((FF_BLOCK, FF_BLOCK, FF_LAST)):
                    off = b * 24
                    with dve.Fori(0, nf // 2) as i:
                        for j in range(2):
                            use = L * (TILES // 2) + ((t0 + off) // 2 + j + 1) + i * 2
                            f = L * (2 * FF_TILES) + (which * FF_TILES + b * FF_BLOCK + j) + i * 2
                            dve.wait_ge(tile_done, ONE + L * TILES + (t0 + off + 2 * j + 1) + i * 4)
                            TT(halves(tmp[:, 4 + j, :]), dps[0][:, :, 0:HALF], rs, ALU.mult).then_inc(slot_free[0], 1)
                            dve.wait_ge(tile_done, ONE + L * TILES + (t0 + off + 2 * j + 2) + i * 4)
                            TT(halves(tmp[:, j, :]), dps[1][:, :, 0:HALF], rs, ALU.mult).then_inc(slot_free[1], 1)
                            dve.wait_ge(slot_free[1], ONE + use)
                            dve.wait_ge(silu_done, f + 1)
                            TT(tmp[:, j, :], tmp[:, j, :], tmp[:, 4 + j, :], ALU.mult).then_inc(ffn_prod, 1)
                            dve.wait_ge(ffn_hi, f + 1)
                            TT(Al[:, bass.ds(i * 2 + j, 1), :], tmp[:, j:j + 1, :],
                               f32(Ah[:, bass.ds(i * 2 + j, 1), :]), ALU.subtract).then_inc(ffn_lo, 1)
                    if b < 2:
                        with dve.Fori(0, 2) as i:
                            for j in range(4):
                                dve.wait_ge(tile_done, ONE + L * TILES + (t0 + off + 2 * nf + j + 1) + i * 4)
                                xs = X[:, bass.ds(i * 4 + j, 1), :].rearrange("p a (b c) -> p (a b) c", b=2)
                                STT(xs, dps[j % 2][:, :, 0:HALF], 0.5, xs, ALU.mult,
                                    ALU.add).then_inc(slot_free[j % 2], 1)
                ssq_start()
                for m in range(KT):
                    t = t0 + off + 2 * nf + m
                    dve.wait_ge(tile_done, ONE + L * TILES + (t + 1))
                    STT(halves(X[:, m, :]), dps[m % 2][:, :, 0:HALF], 0.5, halves(X[:, m, :]), ALU.mult,
                        ALU.add).then_inc(slot_free[m % 2], 1)
                    dve.wait_ge(slot_free[m % 2], ONE + L * (TILES // 2) + (t // 2 + 1))
                    square_sum(slice(m, m + 1))
                    if m == KT - 1:
                        ssq_end()
                    if which:
                        scaled_lo(Hl, Hh, m, par[:, m:m + 1], norm_no + 1)

            def tile(L, t):
                g = MIX_T0 + t
                slot = g % 2
                ps = dps[slot][:, :, 0:HALF]
                free = slot_free[slot]
                silu_no = ([*range(HQ, HF), *range(HF, HI), *range(HG, SMALL), *range(GG, G0[0])])
                if t in silu_no:
                    dve.wait_ge(sig_done, L * 16 + (silu_no.index(t) + 1))
                    if t in range(HF, HI):
                        i = t - HF
                        dve.wait_ge(free, ONE + L * (TILES // 2) + (g // 2 + 1))
                        ch.did(TS(kbuf[:, i, :], kbuf[:, i, :], lbc[:, 4 + i:5 + i], None, ALU.mult))
                        ch.did(TS(R1[0][:, i, :], R1[0][:, i, :], lbc[:, 4 + i:5 + i], lbc[:, i:i + 1],
                                  ALU.mult, ALU.add))
                        return
                    dst = (R0[0][:, t, :] if t < HF else R3[0][:, t - HG, :] if t < SMALL
                           else R3[1][:, t - GG, :])
                    TT(halves(dst), ps, halves(tmp[:, t % 2, :]), ALU.mult).then_inc(free, 1)
                elif t == SMALL:
                    dve.wait_ge(tile_done, ONE + L * TILES + (g + 1))
                    ch.did(dve.tensor_copy(halves(glr[:, :]), dps[slot][0:16, :, 0:HALF]))
                    ch.did(dve.tensor_copy(halves(rows[0:4, 0, :]), dps[slot][32:36, :, 0:HALF]))
                    ch.did(dve.tensor_copy(halves(rows[0:4, 1, :]), dps[slot][64:68, :, 0:HALF]))
                    ch.sync()
                    dve.sem_inc(free, 1)
                    dve.sem_inc(lr_used, 2)

            def tree(ap, op, width, levels, first=1):
                for l in range(first, levels + 1):
                    bs, hf = 1 << l, 1 << (l - 1)
                    v = ap[:, 0:width].rearrange("p (n b) -> p n b", b=bs)
                    ch.link(TT(v[:, :, hf:bs], v[:, :, hf:bs],
                               v[:, :, hf - 1:hf].to_broadcast([HEADS, width // bs, hf]), op))

            def rows_step(L):
                z = setB
                for i in range(2):
                    bias = par[:, P_BG + i:P_BG + i + 1]
                    bank = (SA, SB)[i][:, :, 0:HALF]
                    ch.did(TS(halves(z[:, i, :]), bank, bias, 0.0, ALU.add, ALU.min))
                ch.sync()
                dve.sem_inc(la_1, 1)
                r = rows
                bf = par[0:4, P_BF:P_BF + 1]
                ch.did(TS(r[0:4, 3, :], r[0:4, 1, :], bf, 0.0, ALU.add, ALU.min))
                dve.wait_ge(la_2, L * 1 + 1)
                ch.did(TT(z[:, 4:6, :], z[:, 0:2, :], z[:, 6:8, :], ALU.subtract))
                ch.sync()
                dve.sem_inc(la_3, 1)
                for e in range(2):
                    q = setB[64 * (1 - e):64 * (1 - e) + 64, e:4:2, :]
                    ch.did(dve.memset(q, 0.0))

            def stabiliser(L):
                r = rows
                bi = par[0:4, P_BI:P_BI + 1]
                ch.sync()
                dve.wait_ge(row_y, L + 1)
                ch.link(TT(r[0:4, 1, :], r[0:4, 3, :], r[0:4, 2, :], ALU.subtract))
                tree(r[0:4, 1, :], ALU.add, TOK, S_LEVELS)
                tree(r[0:4, 1, :], ALU.add, SEQ, LEVELS, S_LEVELS + 1)
                ch.link(STT(r[0:4, 4, :], r[0:4, 0, :], bi, r[0:4, 1, :], ALU.add, ALU.subtract))
                ch.link(dve.tensor_copy(r[0:4, 2, :], r[0:4, 4, :]))
                tree(r[0:4, 2, :], ALU.max, TOK, S_LEVELS)
                tree(r[0:4, 2, :], ALU.max, SEQ, LEVELS, S_LEVELS + 1)
                ch.link(dve.memset(mch[:, 0:1], 0.0))
                for c in range(NCH):
                    cs, e = slice(c * CH, (c + 1) * CH), (c + 1) * CH - 1
                    ch.link(TS(r[0:4, 2, cs], r[0:4, 2, cs], mch[:, c:c + 1], None, ALU.max))
                    ch.did(TT(mch[:, c + 1:c + 2], r[0:4, 2, e:e + 1], r[0:4, 1, e:e + 1], ALU.add))
                    ch.sync()
                dve.wait_ge(m_in, L * 32 + 32)
                sv = [r[0:4, i, SEQ:TOK].rearrange("p (b t) -> p b t", t=DEC_T) for i in range(6)]
                m0b = m0[:, :].unsqueeze(2).to_broadcast([HEADS, DEC_B, DEC_T])
                ch.link(TT(sv[2], sv[2], m0b, ALU.max))
                ch.did(TT(mO[:, 1:].unsqueeze(2), sv[2][:, :, 3:4], sv[1][:, :, 3:4], ALU.add))
                ch.did(dve.tensor_copy(mO[:, 0:1], mch[:, NCH:NCH + 1]))
                ch.did(TT(r[0:4, 3, :], r[0:4, 1, :], r[0:4, 2, :], ALU.add))
                ch.sync()
                for c in range(NCH):
                    cs, e = slice(c * CH, (c + 1) * CH), (c + 1) * CH - 1
                    ch.did(TS(r[0:4, 1, cs], r[0:4, 2, cs], -1.0, mch[:, c:c + 1], ALU.mult, ALU.add))
                    ch.did(TS(r[0:4, 0, cs], r[0:4, 4, cs], r[0:4, 2, e:e + 1], None, ALU.subtract))
                ch.did(TT(sv[1], m0b, sv[2], ALU.subtract))
                ch.did(TT(sv[0], sv[4], sv[2][:, :, 3:4].to_broadcast([HEADS, DEC_B, DEC_T]), ALU.subtract))
                ch.did(TS(wrow[0:4, :], r[0:4, 2, :], -1.0, None, ALU.mult))
                ch.sync()
                dve.sem_inc(row_x, 1)

            def qkt_update(br, l):
                w = TOK if l <= S_LEVELS else SEQ
                bs, hf = 1 << l, 1 << (l - 1)

                def bl(ap):
                    return ap[:, :, 0:w].rearrange("p h (n b) -> p h n b", b=bs)

                T = R1[br] if br == 0 else R1[1][:, 0:2, :]
                for e in range(1 if br == 0 else 2):
                    n, ps, hs = (P, slice(0, P), slice(0, 4)) if br == 0 else (64, slice(64 * e, 64 * e + 64),
                                                                              slice(e, 4, 2))
                    q, t = bl(R0[br][ps, hs, :]), bl(T[ps])
                    ch.did(TT(q[:, :, :, hf:bs], q[:, :, :, hf:bs],
                              t[:, :, :, 0:1].to_broadcast([n, t.shape[1], w // bs, hf]), ALU.mult))
                k, t = bl(KB[br]), bl(T)
                ch.did(TT(k[:, :, :, 0:hf], k[:, :, :, 0:hf],
                          t[:, :, :, hf:hf + 1].to_broadcast([P, t.shape[1], w // bs, hf]), ALU.mult))
                ch.sync()
                t = bl(T)
                ch.did(TT(t[:, :, :, 0], t[:, :, :, 0], t[:, :, :, hf], ALU.mult))
                ch.sync()

            def step(L, s):
                kind, br, h = s
                no = L * NSTEPS + STEP_NO[s]
                Q, K, V, Tk, O = R0[br], KB[br], R2[br], KTOK[br], OB[br]
                nt = 2 if br == 1 else 4
                dve.wait_ge(pe_step, ONE + no + 1)
                ch.sync()
                if kind == "rows":
                    rows_step(L)
                elif kind == "cols":
                    ch.did(dve.tensor_copy(colG[:, :], SA[:, 0, 0:16]))
                    ch.did(dve.tensor_copy(colW[:, :], SA[:, 0, 32:48]))
                    ch.did(dve.tensor_copy(colS[:, 0:4], SA[0:SMP, 1, 0:4]))
                    ch.did(dve.tensor_copy(colS[:, 4:8], SA[0:SMP, 1, 32:36]))
                    ch.did(dve.tensor_copy(nS[:, :], SB[:, 0, 0:SMP]))
                elif kind == "d":
                    a = att[:, 2 * h:2 * h + 2, 0:SEQ].rearrange("p h (c t) -> p h c t", t=CH)
                    ch.did(TT(a, SA[:, :, :].rearrange("p h (c t) -> p h c t", t=CH),
                              diag.unsqueeze(1).unsqueeze(1).to_broadcast([P, 2, NCH, CH]), ALU.mult))
                    if h == 0:
                        ch.did(TT(att[0:SMP, :, SEQ:TOK],
                                  SB[0:SMP, 0, 0:4 * SMP].rearrange("p (h t) -> p h t", t=SMP),
                                  diag[0:SMP, 0:SMP].unsqueeze(1).to_broadcast([SMP, 4, SMP]), ALU.mult))
                    else:
                        if br == 0:
                            ch.did(TT(Q, Q, R1[0], ALU.mult))
                        else:
                            for e in range(2):
                                q = Q[64 * e:64 * e + 64, e:4:2, :]
                                ch.did(TT(q, q, R1[1][64 * e:64 * e + 64, 0:2, :], ALU.mult))
                elif kind == "lv":
                    dve.sem_inc(dve_began, 1)
                    bs, hf = 1 << h, 1 << (h - 1)
                    mk = mask(h).rearrange("p (n b) -> p n b", b=bs)[:, :, hf:bs]
                    for s0 in range(0, CH if hf >= 32 else 1, bs):
                        if hf >= 32:
                            n0 = s0 // bs * hf
                            a = att[s0:s0 + hf, :, 0:SEQ].rearrange("p h (c t) -> p h c t", t=CH)
                            src = SA[s0:s0 + hf, :, :].rearrange("p a (b c t) -> p (a b) c t", b=2, c=NCH)
                            ch.did(dve.tensor_copy(a[:, :, :, s0 + hf:s0 + bs], src[:, :, :, n0:n0 + hf]))
                    for i in range(HEADS if hf < 32 else 0):
                        a = att[:, i, 0:SEQ].rearrange("p (c n b) -> p c n b", c=NCH, b=bs)
                        src = SA[:, i // 2, (i % 2) * 256:(i % 2) * 256 + 256]
                        ch.did(dve.copy_predicated(a[:, :, :, hf:bs],
                                                   mk.unsqueeze(1).to_broadcast([P, NCH, CH // bs, hf]),
                                                   src.rearrange("p (c n b) -> p c n b", c=NCH, b=hf)))
                    if h <= S_LEVELS:
                        ch.did(dve.copy_predicated(
                            att[0:SMP, :, SEQ:TOK],
                            mask(h)[0:SMP, 0:SMP].unsqueeze(1).to_broadcast([SMP, 4, SMP]),
                            SB[0:SMP, 0, 0:4 * SMP].rearrange("p (h t) -> p h t", t=SMP)))
                    qkt_update(br, h)
                    if h == LEVELS:
                        T = R1[br][:, 0:nt, :]
                        ch.did(dve.tensor_copy(dec[:, 0:nt, :], T[:, :, 0:SEQ:CH]))
                        ch.did(dve.tensor_copy(decs[:, 0:nt, :], T[:, :, SEQ:TOK:DEC_T]))
                elif kind == "a":
                    for c in range(NCH):
                        cs = slice(c * CH, (c + 1) * CH)
                        ch.did(STT(att[:, h, cs], SA[:, 0, cs], colG[:, c * 4 + h:c * 4 + h + 1],
                                   const[:, C_NEG:C_NEG + 128], ALU.add, ALU.min))
                    ch.did(STT(att[0:SMP, h, SEQ:TOK], SB[0:SMP, 0, 0:32], colS[:, h:h + 1],
                               const[0:SMP, C_NEGS:C_NEGS + 32], ALU.add, ALU.min))
                    ch.sync()
                    dve.sem_inc(d_exp, 1)
                    ch.did(TT(Q[:, h, 0:SEQ], Q[:, h, 0:SEQ], SB[:, 1, :], ALU.mult))
                    ch.did(TT(Q[:, h, SEQ:TOK], Q[:, h, SEQ:TOK], SB[:, 0, 64:96], ALU.mult))
                    ch.did(dve.tensor_copy(dec[:, h, :], SB[:, 1, CH - 1:SEQ:CH]))
                    ch.did(dve.tensor_copy(decs[:, h, :], SB[:, 0, 64 + DEC_T - 1:96:DEC_T]))
                    dve.wait_ge(e_exp, (L * HEADS + h) * 2 + 2)
                    ch.did(TT(att[:, h, 0:SEQ], att[:, h, 0:SEQ], SA[:, 1, :], ALU.mult))
                    ch.did(TT(att[0:SMP, h, SEQ:TOK], att[0:SMP, h, SEQ:TOK], SB[0:SMP, 0, 32:64], ALU.mult))
                elif kind == "u":
                    for i in range(nt):
                        ch.did(dve.tensor_copy(K[:, i, 0:CH], (SA, SB)[i // 2][:, i % 2, 0:CH]))
                    for c in range(1, NCH):
                        ch.sync()
                        for i in range(nt):
                            cs, ps = slice(c * CH, (c + 1) * CH), slice((c - 1) * CH, c * CH)
                            ch.did(STT(K[:, i, cs], K[:, i, ps], dec[:, i, c:c + 1],
                                       (SA, SB)[i // 2][:, i % 2, cs], ALU.mult, ALU.add))
                elif kind == "un":
                    U = SA[:, 0, 0:16].rearrange("p (h c) -> p h c", c=4)
                    ch.link(dve.tensor_copy(nP[:, :, 0:1], U[:, :, 0:1]))
                    for c in range(1, NCH):
                        ch.link(TT(nP[:, :, c:c + 1], nP[:, :, c - 1:c], dec[:, :, c:c + 1], ALU.mult))
                        ch.link(TT(nP[:, :, c:c + 1], nP[:, :, c:c + 1], U[:, :, c:c + 1], ALU.add))
                    v = nO[:, 0:SMP].rearrange("p (b h) -> p b h", h=4)
                    ch.link(TT(v, nS[:, :].rearrange("p (b h) -> p b h", h=4),
                               decs[:, :, :].rearrange("p h b -> p b h"), ALU.mult))
                    ch.link(TT(v, v, SA[:, 0, 64:96].rearrange("p (h b) -> p b h", b=8), ALU.add))
                    ch.did(dve.tensor_copy(nO[:, SMP:SMP + HEADS], nP[:, :, NCH - 1]))
                elif kind == "m":
                    for c in range(1, NCH):
                        cs = slice(c * CH, (c + 1) * CH)
                        ch.did(TS(tmp[:, 5, cs], Q[:, h, cs], nP[:, h, c - 1:c], None, ALU.mult))
                    ch.did(TT(tmp[:, 5, SEQ:TOK].rearrange("p (b t) -> p b t", t=DEC_T),
                              Q[:, h, SEQ:TOK].rearrange("p (b t) -> p b t", t=DEC_T),
                              nS[:, h:SMP:4].unsqueeze(2).to_broadcast([P, DEC_B, DEC_T]), ALU.mult))
                elif kind == "o":
                    if br == 2:
                        nb = tmp[:, 3, :]
                        dve.wait_ge(d_abs, (L * HEADS + h) * 2 + 2)
                        ch.link(TT(nb, nb, tmp[:, 5, :], ALU.max))
                        ch.link(dve.reciprocal(nb, nb))
                        ch.did(TT(O[:, h, 0:SEQ], SA[:, 0, :], nb[:, 0:SEQ], ALU.mult))
                        ch.did(TT(O[:, h, SEQ:TOK], SA[:, 1, 0:SMP], nb[:, SEQ:TOK], ALU.mult))
                        ch.sync()
                        ch.did(TT(tmp[:, 2, :], O[:, h, :], O[:, h, :], ALU.mult))
                    ch.did(TT(vblk[:, :].rearrange("p (b v) -> p b v", v=P),
                              vts[:, h, :].unsqueeze(1).to_broadcast([SMP, DEC_B, P]),
                              const[0:SMP, C_BM:C_BM + 8].unsqueeze(2).to_broadcast([SMP, DEC_B, P]), ALU.mult))
                elif kind == "z":
                    sl = slice(64 * (h % 2), 64 * (h % 2) + 64) if br == 1 else slice(0, P)
                    n = 64 if br == 1 else P
                    st = sst[st_no(br, h) % 2]
                    ch.link(TT(st[sl], st[sl],
                               decs[sl, kt(br, h), :].unsqueeze(2).to_broadcast([n, DEC_B, P]), ALU.mult))
                    TT(st[sl].rearrange("p (a b) v -> p a (b v)", a=2),
                       st[sl].rearrange("p (a b) v -> p a (b v)", a=2), SB[sl, :, :], ALU.add).then_inc(st_upd, 1)
                    idx = L * 12 + (br * 4 + h)
                    dve.wait_ge(h_rs, idx + 1)
                    ch.link(STT(O[:, h, :], O[:, h, :], par[:, P_HN + br:P_HN + br + 1], tmp[:, 5, :],
                                ALU.mult, ALU.mult))
                    TT(O[:, h, :], O[:, h, :], R3[br][:, h, :], ALU.mult).then_inc(h_of, 1)
                    dve.wait_ge(h_hi, idx + 1)
                    TT(OL[br][:, h, :], O[:, h, :], f32(OH[br][:, h, :]), ALU.subtract).then_inc(h_lo, 1)
                    dve.wait_ge(h_lo, idx + 1)
                ch.sync()
                dve.sem_inc(dve_step, 1)

            def branch(L, br, m):
                if br == 0 and m == 0:
                    dve.wait_ge(x_read, L * 32 + 16)
                g = MIX_T0 + (B0, B1, B2)[br][0] + m
                slot = g % 2
                dve.wait_ge(tile_done, ONE + L * TILES + (g + 1))
                gt = MIX_T0 + (G0, G1, G2)[br][0] + m
                dve.wait_ge(slot_free[gt % 2], ONE + L * (TILES // 2) + (gt // 2 + 1))
                dst = X if br == 0 else gates
                TT(halves(dst[:, m, :]), dps[slot][:, :, 0:HALF], halves(gates[:, m, :]),
                   ALU.mult).then_inc(slot_free[slot], 1)
                if br:
                    dve.wait_ge(slot_free[slot], ONE + L * (TILES // 2) + (g // 2 + 1))
                    ins = TT(X[:, m, :], X[:, m, :], gates[:, m, :], ALU.add)
                    if br == 1:
                        ch.did(ins)
                    else:
                        ins.then_inc(mg_f, 1)
                        if m:
                            merged_lo(L, m - 1)
                        if m == KT - 1:
                            merged_lo(L, m)

            def merged_lo(L, m):
                dve.wait_ge(mg_hi, (L * KT + m) + 1)
                TT(Hl[:, m, :], X[:, m, :], f32(Hh[:, m, :]), ALU.subtract).then_inc(mg_lo, 1)

            ch.did(dve.memset(ones[:, :], 1.0))
            ch.did(dve.memset(epsc[:, :], EPS))
            ch.did(dve.memset(wrow[:, :], 0.0))
            dve.wait_ge(par_in, 16)
            ssq_start()
            for m in range(KT):
                dve.wait_ge(x_in[m // 2], 16)
                square_sum(slice(m, m + 1))
                if m == KT - 1:
                    ssq_end()
                scaled_lo(Hl, Hh, m, parL[:, DEPTH - 1, m:m + 1], 0)
            dve.wait_ge(consts_in, 64)
            a, b = lbt[:, 0:4], lbt[:, 4:8]
            ch.did(dve.tensor_copy(lvm[:, :].rearrange("p (a b) -> p a b", a=2), kbuf[:, 0:2, 0:448]))
            ch.link(TT(lbt[:, 16:20], a, b, ALU.max))
            ch.did(TT(lbt[:, 8:12], a, lbt[:, 16:20], ALU.subtract))
            ch.did(TT(lbt[:, 12:16], b, lbt[:, 16:20], ALU.subtract))
            ch.sync()
            dve.sem_inc(const_ready, 1)
            dve.wait_ge(const_ready, 2)
            ch.link(TT(lbt[:, 16:20], lbt[:, 8:12], lbt[:, 12:16], ALU.add))
            ch.link(dve.reciprocal(lbt[:, 16:20], lbt[:, 16:20]))
            ch.did(TT(lbt[:, 8:12], lbt[:, 8:12], lbt[:, 16:20], ALU.mult))
            ch.did(TT(lbt[:, 12:16], lbt[:, 12:16], lbt[:, 16:20], ALU.mult))
            ch.sync()
            ch.link(TT(lbs[:, 1, :], lbt[:, 8:12], lbt[:, 12:16], ALU.add))
            ch.did(TT(lbs[:, 0, :], lbt[:, 8:12], lbt[:, 8:12], ALU.subtract))
            ch.did(TT(lbs[:, 1, :], lbs[:, 1, :], lbt[:, 8:12], ALU.subtract))
            ch.sync()
            with dve.Fori(0, DEPTH) as L:
                outer = ch.loop(L, 1024)
                ch.did(dve.tensor_copy(par[:, 0:31].unsqueeze(1), parL[:, bass.ds(L, 1), :]))
                ch.did(dve.tensor_copy(par[0:16, P_LR:NPAR], const[96:112, bass.ds(L * 256 + C_SEL, 256)]))
                ch.did(dve.tensor_copy(lbc[:, 0:4].unsqueeze(1), lbs[:, bass.ds(L, 1), :]))
                ch.sync()
                ch.did(TS(lbc[:, 4:8], lbc[:, 0:4], -1.0, 1.0, ALU.mult, ALU.add))
                ch.sync()
                ffn(L, 0, L * 3, 0)
                norm(L * 3 + 1, PG["mix"])
                for s in ORDER:
                    if s[0] == "tile":
                        tile(L, s[1])
                    elif s[0] == "branch":
                        branch(L, s[1], s[2])
                    elif s[0] == "stab":
                        stabiliser(L)
                    elif s[0] not in ONE_SIDED:
                        step(L, s)
                ssq_start()
                dve.wait_ge(x_read, L * 32 + 32)
                for m in range(KT):
                    g = MIX_T0 + WO[0] + m
                    dve.wait_ge(tile_done, ONE + L * TILES + (g + 1))
                    TT(halves(X[:, m, :]), dps[g % 2][:, :, 0:HALF], halves(X[:, m, :]),
                       ALU.add).then_inc(slot_free[g % 2], 1)
                    dve.wait_ge(slot_free[g % 2], ONE + L * (TILES // 2) + (g // 2 + 1))
                    square_sum(slice(m, m + 1))
                    if m == KT - 1:
                        ssq_end()
                    scaled_lo(Ml, Mh, m, par[:, PG["ffn2"] + m:PG["ffn2"] + m + 1], L * 3 + 2)
                dve.wait_ge(tile_done, ONE + L * TILES + FFN2_T0)
                dve.sem_inc(slot_free[1], 1)
                ffn(L, FFN2_T0, L * 3 + 2, 1)
                dve.wait_ge(norm_lo, L * (3 * KT) + 4 * KT)
                ch.end(outer, 1024, DEPTH)
            dve.wait_ge(rs_ready, 3 * DEPTH + 1)
            for k in range(KT):
                STT(X[:, k, :], X[:, k, :], fg[:, k:k + 1], tmp[:, 2, :], ALU.mult, ALU.mult).then_inc(y_ready, 1)


def _tiles(w):
    return w.reshape(w.shape[0] // P, P, w.shape[1] // P, P).transpose(0, 2, 1, 3)


def weight_stream(a):
    out = np.zeros((DEPTH, PIECES, P, 8, P), np.float32)
    for l in range(DEPTH):
        n = 0

        def put(tiles, at=0):
            nonlocal n
            out[l, n, :, at:at + tiles.shape[0], :] = tiles.transpose(1, 0, 2)

        def ffn(up, down):
            nonlocal n
            up, down = _tiles(up), _tiles(down)
            for f0, nf in ((0, FF_BLOCK), (FF_BLOCK, FF_BLOCK), (2 * FF_BLOCK, FF_LAST)):
                for f in range(f0, f0 + nf):
                    put(up[:, f]); n += 1
                    put(up[:, FF_TILES + f]); n += 1
                for m in range(KT):
                    put(down[f0:f0 + nf, m]); n += 1

        ffn(a["ffn1_w_up"][l], a["ffn1_w_down"][l])
        w = a["w_in"][l]
        sizes = [512] * 4 + [256, 256, 512, 512, 16] + [512] * 4 + [4, 4, 3072]
        at = np.cumsum([0] + sizes)
        part = [w[:, at[i]:at[i + 1]] for i in range(len(sizes))]
        small = np.zeros((D_MODEL, P), np.float32)
        small[:, 0:16], small[:, 32:36], small[:, 64:68] = part[8], part[13], part[14]

        def proj(x):
            nonlocal n
            for i in range(x.shape[1] // P):
                put(_tiles(x)[:, i]); n += 1

        def gate(b):
            proj(part[15][:, b * D_MODEL:(b + 1) * D_MODEL])

        def branch(b):
            nonlocal n
            t = _tiles(a["w_branch"][l, b])
            for m in range(0, KT, 2):
                put(t[:, m]); put(t[:, m + 1], 4); n += 1

        for i in (0, 1, 2, 3):
            proj(part[i])
        proj(small)
        for i in (4, 5, 6, 7):
            proj(part[i])
        gate(0); branch(0)
        for i in (9, 10, 11, 12):
            proj(part[i])
        gate(1); branch(1); gate(2); branch(2)
        proj(a["w_out"][l])
        n += 1
        ffn(a["ffn2_w_up"][l], a["ffn2_w_down"][l])
        assert n == PIECES
    return out.reshape(DEPTH * PIECES, P, 1024)


def constants():
    c = np.zeros((P, NCONST), np.float32)
    m = np.zeros((P, LEVELS * P), np.float32)
    i = np.arange(P)
    s, t = i[:, None], i[None, :]
    c[:, C_ID:C_ID + P] = s == t
    c[:, C_DIAG:C_DIAG + P] = s == t
    for l in range(1, LEVELS + 1):
        b, hf = 1 << l, 1 << (l - 1)
        m[:, (l - 1) * P:l * P] = (s // b == t // b) & (s % b < hf) & (t % b >= hf)
    c[:, C_NEG:C_NEG + P] = np.where(s <= t, 0.0, -1e30)
    c[0:SMP, C_NEGS:C_NEGS + SMP] = np.where((s <= t) & (s // DEC_T == t // DEC_T), 0.0, -1e30)[0:SMP, 0:SMP]
    for q in range(3):
        for h in range(HEADS):
            c[32 * q + h, C_SEL + h * P:C_SEL + (h + 1) * P] = 1.0
    c[0:SMP, C_BM:C_BM + DEC_B] = np.arange(SMP)[:, None] // DEC_T == np.arange(DEC_B)[None, :]
    return c, m


def kernel(**inputs):
    import concourse.bacc as bacc
    from concourse.bass_utils import run_bass_kernel_spmd

    a = {k: np.asarray(v) for k, v in inputs.items()}

    def cols(v, n):
        return v.reshape(DEPTH, n, P).transpose(2, 0, 1)

    par = np.zeros((P, DEPTH, P_LR), np.float32)
    for l in range(DEPTH):
        par[:, l, 0:8] = cols(a["ffn1_norm"], 8)[:, (l + 1) % DEPTH]
    par[:, :, 8:16] = cols(a["mix_norm"], 8)
    par[:, :, 16:24] = cols(a["ffn2_norm"], 8)
    for i, name in enumerate(("hgrn_out_norm", "gla_out_norm", "mlstm_out_norm")):
        par[:, :, P_HN + i] = a[name].T
    par[:, :, P_BG:P_BG + 2] = cols(a["gla_b_gate"], 2)
    par[0:4, :, P_BI], par[0:4, :, P_BF] = a["mlstm_b_i"].T, a["mlstm_b_f"].T
    const, lvm = constants()
    const[96:112, C_SEL:C_SEL + 512] = a["gla_w_gate_lr"].transpose(1, 0, 2).reshape(16, 512)
    xs = np.concatenate([a["x_prompt"].reshape(SEQ, D_MODEL), a["x_sample"].reshape(SMP, D_MODEL)])
    arrays = {
        "wst": weight_stream(a),
        "xT": np.ascontiguousarray(xs.T.reshape(KT, P, TOK).transpose(1, 0, 2)),
        "par": par,
        "lb": np.ascontiguousarray(cols(a["hgrn_lb_raw"], 4).reshape(P, 8)),
        "const": const,
        "lvm": lvm.reshape(P, 2, 448),
        "fg": np.ascontiguousarray(a["final_norm"].reshape(KT, P).T),
        "st_h": a["state_hgrn"],
        "st_g": a["state_gla"].reshape(DEPTH, DEC_B, 2, P, P),
        "st_c": a["state_mlstm_C"],
        "st_n": a["state_mlstm_n"].reshape(DEPTH, SMP, P),
        "st_m": np.ascontiguousarray(a["state_mlstm_m"].transpose(0, 2, 1)),
    }
    nc = bacc.Bacc("TRN2", target_bir_lowering=False, num_devices=1)
    args = [nc.dram_tensor(k, v.shape, mybir.dt.from_np(v.dtype), kind="ExternalInput").ap() for k, v in arrays.items()]
    outs = {
        "yT": (P, KT, TOK), "p_h": (DEPTH, 4, P, P), "p_g": (DEPTH, 2, P, P), "p_c": (DEPTH, 4, P, P),
        "p_n": (DEPTH, 4, P), "s_h": (DEPTH, DEC_B, 4, P, P),
        "s_g": (DEPTH, DEC_B, 2, P, P), "s_c": (DEPTH, DEC_B, 4, P, P), "s_n": (DEPTH, SMP, P),
        "s_m": (DEPTH, 4, 1 + DEC_B),
    }
    args += [nc.dram_tensor(k, s, F32, kind="ExternalOutput").ap() for k, s in outs.items()]
    args.append(nc.dram_tensor("x_keep", (P, KT, TOK), F32, kind="Internal").ap())
    build(nc, *args)
    r = run_bass_kernel_spmd(nc, [arrays], core_ids=[0]).results[0]
    y = r["yT"].transpose(2, 1, 0).reshape(TOK, D_MODEL)
    return (y[0:SEQ].reshape(1, SEQ, D_MODEL), y[SEQ:].reshape(DEC_B, DEC_T, D_MODEL),
            r["p_h"].reshape(DEPTH, 1, 4, P, P), r["p_g"].reshape(DEPTH, 1, 4, 64, P),
            r["p_c"].reshape(DEPTH, 1, 4, P, P), r["p_n"].reshape(DEPTH, 1, 4, P),
            r["s_m"][:, :, 0].reshape(DEPTH, 1, 4), r["s_h"], r["s_g"].reshape(DEPTH, DEC_B, 4, 64, P), r["s_c"],
            r["s_n"].reshape(DEPTH, DEC_B, 4, P),
            r["s_m"][:, :, 1:].transpose(0, 2, 1))
```
